# Optimizing a Trainium2 kernel written in Bass

```python
import jax, jax.numpy as jnp
from jax import lax
import numpy as np
import math

D_MODEL = 2048
BATCH = 1
SEQ = 256
DEPTH = 2

CTX_LEN = 256
GRID_W = 64
D_MIX = D_MODEL
D_CONV = D_MIX // 2
D_RET = D_MIX - D_CONV
RET_HEADS = 8
RET_HEAD_DIM = D_RET // RET_HEADS
CONV_WIDTH = 3
CHUNK = 128
D_IN = 4 * D_CONV + 4 * D_RET
ROPE_BASE = 10000.0
RET_DECAY_OFFSET = 5.0
EPS = 1e-6


def _rmsnorm(x, w):
    xf = x.astype(jnp.float32)
    y = xf * lax.rsqrt(jnp.mean(xf * xf, axis=-1, keepdims=True) + EPS)
    return (y * w.astype(jnp.float32)).astype(x.dtype)

def _split_in(u):
    idx = [D_CONV, 2 * D_CONV, 3 * D_CONV, 4 * D_CONV,
           4 * D_CONV + D_RET, 4 * D_CONV + 2 * D_RET, 4 * D_CONV + 3 * D_RET]
    return jnp.split(u, idx, axis=-1)

def _short_conv(u, w):
    up = jnp.pad(u, ((0, 0), (1, 1), (0, 0)))
    return up[:, :-2] * w[0] + up[:, 1:-1] * w[1] + up[:, 2:] * w[2]

def _conv_branch(h, b, c, z, conv_w, norm_w):
    y = b * _short_conv(c * h, conv_w)
    return jax.nn.silu(z) * _rmsnorm(y, norm_w)

def _heads(t):
    b, l, _ = t.shape
    return t.reshape(b, l, RET_HEADS, RET_HEAD_DIM).transpose(0, 2, 1, 3)

def _rope_1d(x, pos):
    f = x.shape[-1] // 2
    inv = ROPE_BASE ** (-jnp.arange(f, dtype=jnp.float32) / f)
    ang = pos.astype(jnp.float32)[:, None] * inv[None, :]
    cos, sin = jnp.cos(ang), jnp.sin(ang)
    x1, x2 = x[..., :f], x[..., f:]
    return jnp.concatenate([x1 * cos - x2 * sin, x1 * sin + x2 * cos], axis=-1).astype(x.dtype)

def _axial_rope(x, row_pos, col_pos):
    half = x.shape[-1] // 2
    return jnp.concatenate([_rope_1d(x[..., :half], row_pos),
                            _rope_1d(x[..., half:], col_pos)], axis=-1)

def _chunk_retention(q, k, v, lg, s0):
    b, h, l, dk = q.shape
    n = l // CHUNK
    qc = q.reshape(b, h, n, CHUNK, dk)
    kc = k.reshape(b, h, n, CHUNK, dk)
    vc = v.reshape(b, h, n, CHUNK, v.shape[-1])
    pos = jnp.arange(CHUNK, dtype=jnp.float32)
    diff = pos[:, None] - pos[None, :]
    dmask = jnp.where(diff >= 0, jnp.exp(lg[:, None, None] * jnp.maximum(diff, 0.0)[None]), 0.0)
    scores = jnp.einsum('bhnid,bhnjd->bhnij', qc, kc) * dmask[None, :, None]
    intra = jnp.einsum('bhnij,bhnje->bhnie', scores, vc)
    k_decay = jnp.exp(lg[:, None] * (CHUNK - 1 - pos)[None])
    q_decay = jnp.exp(lg[:, None] * (pos + 1.0)[None])
    chunk_decay = jnp.exp(lg * CHUNK)
    chunk_kv = jnp.einsum('bhnjd,hj,bhnje->nbhde', kc, k_decay, vc)

    def step(s, kv):
        return chunk_decay[None, :, None, None] * s + kv, s

    _, s_prev = lax.scan(step, s0, chunk_kv)
    inter = jnp.einsum('bhnid,hi,nbhde->bhnie', qc, q_decay, s_prev)
    return (intra + inter).reshape(b, h, l, -1)

def _bidir_retention(q, k, v, lg_f, lg_b, s0_f, s0_b):
    o_f = _chunk_retention(q, k, v, lg_f, s0_f)
    flip = lambda t: jnp.flip(t, axis=2)
    o_b = _chunk_retention(flip(q), flip(k), flip(v), lg_b, s0_b)
    return o_f + flip(o_b)

def _context_states(k, v, lg_f, lg_b):
    lc = k.shape[2]
    t = jnp.arange(lc, dtype=jnp.float32)
    w_f = jnp.exp(lg_f[:, None] * (lc - 1.0 - t)[None])
    w_b = jnp.exp(lg_b[:, None] * t[None])
    s_f = jnp.einsum('bhtd,ht,bhte->bhde', k, w_f, v)
    s_b = jnp.einsum('bhtd,ht,bhte->bhde', k, w_b, v)
    return s_f, s_b

def _ret_out(o, z, gn_w):
    of = o.astype(jnp.float32)
    mu = jnp.mean(of, axis=-1, keepdims=True)
    var = jnp.mean(jnp.square(of - mu), axis=-1, keepdims=True)
    on = (of - mu) * lax.rsqrt(var + EPS)
    b, h, l, d = on.shape
    on = on.transpose(0, 2, 1, 3).reshape(b, l, h * d) * gn_w.astype(jnp.float32)
    return jax.nn.silu(z) * on.astype(z.dtype)

def _layer(x, ctx, c, c_ctx, norm_w, w_mod, b_mod, w_in, conv_w, conv_norm_w, ret_norm_w,
           decay_f, decay_b, w_out, row_pos, col_pos, update_ctx):
    d = D_MODEL
    lg_f = -jnp.exp(decay_f.astype(jnp.float32))
    lg_b = -jnp.exp(decay_b.astype(jnp.float32))
    k_scale = RET_HEAD_DIM ** -0.5

    shift, scale, gate = jnp.split(jax.nn.silu(c) @ w_mod + b_mod, 3, axis=-1)
    hx = _rmsnorm(x, norm_w) * (1 + scale[:, None]) + shift[:, None]
    a_h, a_b, a_c, a_z, q, k, v, r_z = _split_in(hx @ w_in)

    n_mod = 3 if update_ctx else 2
    mod_c = jax.nn.silu(c_ctx) @ w_mod[:, :n_mod * d] + b_mod[:n_mod * d]
    hc = _rmsnorm(ctx, norm_w) * (1 + mod_c[d:2 * d]) + mod_c[:d]
    if update_ctx:
        ca_h, ca_b, ca_c, ca_z, cq, ck, cv, cr_z = _split_in(hc @ w_in)
    else:
        kv0 = 4 * D_CONV + D_RET
        ck, cv = jnp.split(hc @ w_in[:, kv0:kv0 + 2 * D_RET], 2, axis=-1)
    ck_h = _heads(ck) * k_scale
    cv_h = _heads(cv)
    s_f, s_b = _context_states(ck_h, cv_h, lg_f, lg_b)

    q_h = _axial_rope(_heads(q), row_pos, col_pos)
    k_h = _axial_rope(_heads(k), row_pos, col_pos) * k_scale
    o = _bidir_retention(q_h, k_h, _heads(v), lg_f, lg_b, s_f, s_b)
    y_ret = _ret_out(o, r_z, ret_norm_w)
    y_conv = _conv_branch(a_h, a_b, a_c, a_z, conv_w, conv_norm_w)
    x = x + gate[:, None] * (jnp.concatenate([y_conv, y_ret], axis=-1) @ w_out)

    if update_ctx:
        zeros = jnp.zeros_like(s_f)
        oc = _bidir_retention(_heads(cq), ck_h, cv_h, lg_f, lg_b, zeros, zeros)
        yc_ret = _ret_out(oc, cr_z, ret_norm_w)
        yc_conv = _conv_branch(ca_h, ca_b, ca_c, ca_z, conv_w, conv_norm_w)
        ctx = ctx + mod_c[2 * d:] * (jnp.concatenate([yc_conv, yc_ret], axis=-1) @ w_out)
    return x, ctx

def first_inputs(seed: int = 0) -> dict:
    key = jax.random.key(seed)
    ks = jax.random.split(key, 16)
    f32 = jnp.float32
    nrm = lambda k, s: jax.random.normal(k, s, f32)
    base = jnp.log(-jnp.log1p(-(2.0 ** -(RET_DECAY_OFFSET + jnp.arange(RET_HEADS, dtype=f32)))))
    return {
        "x": nrm(ks[0], (BATCH, SEQ, D_MODEL)),
        "c": nrm(ks[1], (BATCH, D_MODEL)),
        "ctx": nrm(ks[2], (BATCH, CTX_LEN, D_MODEL)),
        "c_ctx": nrm(ks[3], (D_MODEL,)),
        "norm_w": 1.0 + 0.05 * nrm(ks[4], (DEPTH, D_MODEL)),
        "w_mod": nrm(ks[5], (DEPTH, D_MODEL, 3 * D_MODEL)) * (0.5 * D_MODEL ** -0.5),
        "b_mod": 0.02 * nrm(ks[6], (DEPTH, 3 * D_MODEL)),
        "w_in": nrm(ks[7], (DEPTH, D_MODEL, D_IN)) * D_MODEL ** -0.5,
        "conv_w": nrm(ks[8], (DEPTH, CONV_WIDTH, D_CONV)) * CONV_WIDTH ** -0.5,
        "conv_norm_w": 1.0 + 0.05 * nrm(ks[9], (DEPTH, D_CONV)),
        "ret_norm_w": 1.0 + 0.05 * nrm(ks[10], (DEPTH, D_RET)),
        "ret_decay_f": base[None] + 0.05 * nrm(ks[11], (DEPTH, RET_HEADS)),
        "ret_decay_b": base[None] + 0.05 * nrm(ks[12], (DEPTH, RET_HEADS)),
        "w_out": nrm(ks[13], (DEPTH, D_MIX, D_MODEL)) * D_MIX ** -0.5,
        "final_norm_w": 1.0 + 0.05 * nrm(ks[14], (D_MODEL,)),
    }

def first_block(x, c, ctx, c_ctx, norm_w, w_mod, b_mod, w_in, conv_w, conv_norm_w, ret_norm_w,
              ret_decay_f, ret_decay_b, w_out, final_norm_w):
    seq = x.shape[1]
    rows = seq // GRID_W
    row_pos = jnp.repeat(jnp.arange(rows), GRID_W)
    col_pos = jnp.tile(jnp.arange(GRID_W), rows)
    for layer in range(DEPTH):
        x, ctx = _layer(x, ctx, c, c_ctx, norm_w[layer], w_mod[layer], b_mod[layer], w_in[layer],
                        conv_w[layer], conv_norm_w[layer], ret_norm_w[layer],
                        ret_decay_f[layer], ret_decay_b[layer], w_out[layer],
                        row_pos, col_pos, layer < DEPTH - 1)
    return _rmsnorm(x, final_norm_w)


DEPTH_2 = 1

SSM_HEAD_DIM = 64
SSM_HEADS = D_MODEL // SSM_HEAD_DIM
D_SSM = SSM_HEADS * SSM_HEAD_DIM
SSM_GROUPS = 8
HEADS_PER_GROUP = SSM_HEADS // SSM_GROUPS
D_STATE = 128
CONV_WIDTH_2 = 4
SSD_CHUNK = 128
D_XBC = D_SSM + 2 * SSM_GROUPS * D_STATE

ATT_HEAD_DIM = 128
ATT_HEADS = D_MODEL // ATT_HEAD_DIM
D_ATT = ATT_HEADS * ATT_HEAD_DIM
DILATION_PAIRS = ((128, 1), (512, 4), (2048, 16))
ATT_BLOCK = 128

D_MIX_2 = D_SSM + D_ATT
IN_SPLITS = (D_SSM,
             D_SSM + D_XBC,
             D_SSM + D_XBC + SSM_HEADS,
             D_SSM + D_XBC + SSM_HEADS + D_ATT,
             D_SSM + D_XBC + SSM_HEADS + 2 * D_ATT)
D_IN_PROJ = D_SSM + D_XBC + SSM_HEADS + 3 * D_ATT
D_FF = 4 * D_MODEL


def rmsnorm(x, w):
    xf = x.astype(jnp.float32)
    xf = xf * lax.rsqrt(jnp.mean(xf * xf, axis=-1, keepdims=True) + EPS)
    return (xf * w.astype(jnp.float32)).astype(x.dtype)

def causal_depthwise_conv(u, w, b):
    out = lax.conv_general_dilated(
        u, w[:, None, :].astype(u.dtype), window_strides=(1,),
        padding=[(CONV_WIDTH_2 - 1, 0)],
        dimension_numbers=('NWC', 'WIO', 'NWC'),
        feature_group_count=u.shape[-1])
    return out + b.astype(u.dtype)

def ssd_chunked(xh, dt, a, bm, cm):
    b_, s_ = xh.shape[:2]
    nc = s_ // SSD_CHUNK

    def chunk(t):
        return t.reshape((b_, nc, SSD_CHUNK) + t.shape[2:])

    xc, dtc, bc, cc = chunk(xh), chunk(dt), chunk(bm), chunk(cm)
    a_cs = jnp.cumsum(dtc * a, axis=2).transpose(0, 1, 3, 4, 2)
    causal = jnp.tril(jnp.ones((SSD_CHUNK, SSD_CHUNK), dtype=bool))
    decay_in = jnp.exp(jnp.where(causal, a_cs[..., :, None] - a_cs[..., None, :], -jnp.inf))
    cb = jnp.einsum('bcign,bcjgn->bcgij', cc, bc)
    xdt = xc * dtc[..., None]
    y_diag = jnp.einsum('bcgrij,bcjgrp->bcigrp', cb[:, :, :, None] * decay_in, xdt)

    decay_to_end = jnp.exp(a_cs[..., -1:] - a_cs)
    states = jnp.einsum('bcjgn,bcgrj,bcjgrp->bcgrpn', bc, decay_to_end, xdt)
    chunk_decay = jnp.exp(a_cs[..., -1])

    def step(h, inp):
        st, dec = inp
        return h * dec[..., None, None] + st, h

    h0 = jnp.zeros(states.shape[:1] + states.shape[2:], jnp.float32)
    _, prev = lax.scan(step, h0, (jnp.swapaxes(states, 0, 1), jnp.swapaxes(chunk_decay, 0, 1)))
    prev = jnp.swapaxes(prev, 0, 1)
    y_off = jnp.einsum('bcign,bcgrpn,bcgri->bcigrp', cc, prev, jnp.exp(a_cs))
    return (y_diag + y_off).reshape(xh.shape)

def dilated_window_attention(q, k, v, window, dilation):
    b_, s_, h_, d_ = q.shape
    sd = s_ // dilation
    reach = window // dilation
    nb = -(-sd // ATT_BLOCK)
    lp = nb * ATT_BLOCK
    bd = b_ * dilation

    def decimate(t):
        t = t.reshape(b_, sd, dilation, h_, d_).transpose(0, 2, 1, 3, 4)
        t = t.reshape(bd, sd, h_, d_)
        return jnp.pad(t, ((0, 0), (0, lp - sd), (0, 0), (0, 0)))

    def with_prev(t):
        t = jnp.pad(t, ((0, 0), (ATT_BLOCK, 0), (0, 0), (0, 0)))
        t = t.reshape(bd, nb + 1, ATT_BLOCK, h_, d_)
        return jnp.concatenate([t[:, :-1], t[:, 1:]], axis=2)

    qb = decimate(q).reshape(bd, nb, ATT_BLOCK, h_, d_)
    kb = with_prev(decimate(k))
    vb = with_prev(decimate(v))
    s = jnp.einsum('bnqhd,bnkhd->bnhqk', qb, kb)
    qi = jnp.arange(ATT_BLOCK)[:, None]
    kj = jnp.arange(2 * ATT_BLOCK)[None, :]
    dist = ATT_BLOCK + qi - kj
    key_pos = (jnp.arange(nb)[:, None, None] - 1) * ATT_BLOCK + kj[None]
    mask = (dist >= 0) & (dist <= reach) & (key_pos >= 0)
    s = jnp.where(mask[None, :, None], s, -jnp.inf)
    m = jnp.max(s, axis=-1, keepdims=True)
    p = jnp.exp(s - m)
    den = jnp.sum(p, axis=-1)
    o = jnp.einsum('bnhqk,bnkhd->bnqhd', p, vb) / jnp.swapaxes(den, 2, 3)[..., None]
    lse = jnp.swapaxes(m[..., 0] + jnp.log(den), 2, 3)

    def undecimate(t):
        t = t.reshape((bd, lp) + t.shape[3:])[:, :sd]
        t = t.reshape((b_, dilation, sd) + t.shape[2:])
        return jnp.moveaxis(t, 1, 2).reshape((b_, s_) + t.shape[3:])

    return undecimate(o), undecimate(lse)

def hybrid_mixer(u, w_in, conv_w, conv_b, dt_bias, a_log, d_skip, ssm_norm_w, w_out):
    b_, s_, _ = u.shape
    f32 = jnp.float32
    proj = jnp.einsum('bsd,de->bse', u, w_in)
    z, xbc, dt_raw, q, k, v = jnp.split(proj, IN_SPLITS, axis=-1)

    xbc = jax.nn.silu(causal_depthwise_conv(xbc, conv_w, conv_b))
    xs, bm, cm = jnp.split(xbc, (D_SSM, D_SSM + SSM_GROUPS * D_STATE), axis=-1)
    xh = xs.astype(f32).reshape(b_, s_, SSM_GROUPS, HEADS_PER_GROUP, SSM_HEAD_DIM)
    dt = jax.nn.softplus(dt_raw.astype(f32) + dt_bias.astype(f32))
    dt = dt.reshape(b_, s_, SSM_GROUPS, HEADS_PER_GROUP)
    a = -jnp.exp(a_log.astype(f32)).reshape(SSM_GROUPS, HEADS_PER_GROUP)
    bm = bm.astype(f32).reshape(b_, s_, SSM_GROUPS, D_STATE)
    cm = cm.astype(f32).reshape(b_, s_, SSM_GROUPS, D_STATE)
    y = ssd_chunked(xh, dt, a, bm, cm)
    y = y + d_skip.astype(f32).reshape(SSM_GROUPS, HEADS_PER_GROUP)[:, :, None] * xh
    yg = y.reshape(b_, s_, SSM_GROUPS, -1) * jax.nn.silu(z.astype(f32)).reshape(b_, s_, SSM_GROUPS, -1)
    yg = yg * lax.rsqrt(jnp.mean(yg * yg, axis=-1, keepdims=True) + EPS)
    y_ssm = (yg.reshape(b_, s_, D_SSM) * ssm_norm_w.astype(f32)).astype(u.dtype)

    qh = q.astype(f32).reshape(b_, s_, ATT_HEADS, ATT_HEAD_DIM) * (ATT_HEAD_DIM ** -0.5)
    kh = k.astype(f32).reshape(b_, s_, ATT_HEADS, ATT_HEAD_DIM)
    vh = v.astype(f32).reshape(b_, s_, ATT_HEADS, ATT_HEAD_DIM)
    outs, lses = [], []
    for window, dilation in DILATION_PAIRS:
        o, l = dilated_window_attention(qh, kh, vh, window, dilation)
        outs.append(o)
        lses.append(l)
    wts = jax.nn.softmax(jnp.stack(lses, axis=0), axis=0)
    y_att = jnp.einsum('ibsh,ibshd->bshd', wts, jnp.stack(outs, axis=0))
    y_att = y_att.reshape(b_, s_, D_ATT).astype(u.dtype)

    y_mix = jnp.concatenate([y_ssm, y_att], axis=-1)
    return jnp.einsum('bse,ed->bsd', y_mix, w_out)

def squared_relu_mlp(u, w_up, w_down):
    hdn = jax.nn.relu(jnp.einsum('bsd,df->bsf', u, w_up))
    return jnp.einsum('bsf,fd->bsd', hdn * hdn, w_down)

def second_inputs(seed: int = 0) -> dict:
    key = jax.random.key(seed)
    ks = jax.random.split(key, 16)
    L = DEPTH_2

    def gain(k, n):
        return 1.0 + 0.1 * jax.random.normal(k, (L, n), jnp.float32)

    dt0 = jnp.exp(jax.random.uniform(ks[5], (L, SSM_HEADS), jnp.float32,
                                     math.log(1e-3), math.log(1e-1)))
    dt_bias = dt0 + jnp.log(-jnp.expm1(-dt0))
    return {
        "x": jax.random.normal(ks[0], (BATCH, SEQ, D_MODEL), jnp.float32),
        "norm_mix_pre": gain(ks[1], D_MODEL),
        "w_in": jax.random.normal(ks[2], (L, D_MODEL, D_IN_PROJ), jnp.float32) * D_MODEL ** -0.5,
        "conv_w": jax.random.normal(ks[3], (L, CONV_WIDTH_2, D_XBC), jnp.float32) * CONV_WIDTH_2 ** -0.5,
        "conv_b": 0.01 * jax.random.normal(ks[4], (L, D_XBC), jnp.float32),
        "dt_bias": dt_bias,
        "a_log": jnp.log(jax.random.uniform(ks[6], (L, SSM_HEADS), jnp.float32, 1.0, 16.0)),
        "d_skip": gain(ks[7], SSM_HEADS),
        "ssm_norm_w": gain(ks[8], D_SSM),
        "w_out": jax.random.normal(ks[9], (L, D_MIX_2, D_MODEL), jnp.float32) * D_MIX_2 ** -0.5,
        "norm_mix_post": gain(ks[10], D_MODEL),
        "norm_mlp_pre": gain(ks[11], D_MODEL),
        "w_up": jax.random.normal(ks[12], (L, D_MODEL, D_FF), jnp.float32) * D_MODEL ** -0.5,
        "w_down": jax.random.normal(ks[13], (L, D_FF, D_MODEL), jnp.float32) * D_FF ** -0.5,
        "norm_mlp_post": gain(ks[14], D_MODEL),
    }

def second_block(x, norm_mix_pre, w_in, conv_w, conv_b, dt_bias, a_log, d_skip, ssm_norm_w,
              w_out, norm_mix_post, norm_mlp_pre, w_up, w_down, norm_mlp_post):
    h = x
    for i in range(DEPTH_2):
        mix = hybrid_mixer(rmsnorm(h, norm_mix_pre[i]), w_in[i], conv_w[i], conv_b[i],
                           dt_bias[i], a_log[i], d_skip[i], ssm_norm_w[i], w_out[i])
        h = h + rmsnorm(mix, norm_mix_post[i])
        ff = squared_relu_mlp(rmsnorm(h, norm_mlp_pre[i]), w_up[i], w_down[i])
        h = h + rmsnorm(ff, norm_mlp_post[i])
    return h


def setup_inputs(seed=0):
    out = dict(first_inputs(seed))
    for name, value in second_inputs(seed + 1).items():
        if name != "x":
            out[name + "_2"] = value
    return out


def reference(
    x, c, ctx, c_ctx, norm_w, w_mod, b_mod, w_in, conv_w, conv_norm_w, ret_norm_w, ret_decay_f,
    ret_decay_b, w_out, final_norm_w, norm_mix_pre_2, w_in_2, conv_w_2, conv_b_2, dt_bias_2,
    a_log_2, d_skip_2, ssm_norm_w_2, w_out_2, norm_mix_post_2, norm_mlp_pre_2, w_up_2, w_down_2,
    norm_mlp_post_2,
):
    x = first_block(
        x, c, ctx, c_ctx, norm_w, w_mod, b_mod, w_in, conv_w, conv_norm_w, ret_norm_w,
        ret_decay_f, ret_decay_b, w_out, final_norm_w,
    )
    return second_block(
        x, norm_mix_pre_2, w_in_2, conv_w_2, conv_b_2, dt_bias_2, a_log_2, d_skip_2,
        ssm_norm_w_2, w_out_2, norm_mix_post_2, norm_mlp_pre_2, w_up_2, w_down_2,
        norm_mlp_post_2,
    )


_drawn_inputs = setup_inputs


def setup_inputs(seed=0):
    import zlib

    import numpy as np

    out = dict(_drawn_inputs(seed))
    spreads = {}
    factors = {'conv_norm_w': 4.098, 'ret_norm_w': 4.219, 'conv_b_2': 5.479}
    for name, (base, spread) in spreads.items():
        noise = np.random.default_rng([zlib.crc32(name.encode()), seed]).standard_normal(out[name].shape)
        drawn = base * np.exp(spread * noise) if base else spread * noise
        out[name] = __import__('jax').numpy.asarray(drawn.astype(out[name].dtype))
    for name, factor in factors.items():
        out[name] = (out[name] * factor).astype(out[name].dtype)
    return out
```

```python
from contextlib import ExitStack

import concourse.bass as bass
import numpy as np
from concourse import mybir

P = 128
TOK = 256
D = 2048
KT = D // P
HEADS = 8
SSM_HEADS = 32
SSM_GROUPS = 8
ATT_HEADS = 16
FF = 4 * D
EPS = 1e-6
CHUNK_K = 8
WCOL = 256
SLOTS = 4

W_SCALE = 256.0
A_SCALE = 16.0
UNSCALE = 1.0 / (W_SCALE * A_SCALE)
HEAD_SCALE = float(P) ** -0.5

F32 = mybir.dt.float32
F16 = mybir.dt.float16
BF16 = mybir.dt.bfloat16
ALU = mybir.AluOpType
ACT = mybir.ActivationFunctionType
AX = mybir.AxisListType

UNITS = dict(mod=16, conv0=32, ret0=32, out0=8, conv1=16, ret1=16, out1=8,
             att=24, ssd=24, mixout=16, up=32, down=32)
GROUPS = dict(UNITS, mixout=8, down=8)
U0, G0, _u, _g = {}, {}, 0, 0
for _name in UNITS:
    U0[_name], G0[_name] = _u, _g
    _u += UNITS[_name]
    _g += GROUPS[_name]
N_UNITS = _u
N_CHUNKS = 2 * N_UNITS

PCOLS = {}
_c = 0
for _name, _n in (("norm_w", 2 * KT), ("b_mod", 2 * 48), ("conv_w", 2 * 3 * 8), ("conv_norm_w", 16),
                  ("ret_norm_w", 16), ("final_norm_w", KT), ("mix_pre", KT), ("ssm_norm_w", KT),
                  ("mix_post", KT), ("mlp_pre", KT), ("mlp_post", KT), ("conv_w2", 4 * 32),
                  ("conv_b2", 32), ("c", KT), ("c_ctx", KT)):
    PCOLS[_name] = _c
    _c += _n
N_PCOLS = _c

RES = dict(out0=1, out1=2, final=3, mix=4, mlp=5)


class Chain:

    def __init__(self, eng, sem):
        self.eng, self.sem, self.base, self.k, self.i, self.per = eng, sem, 0, 0, 0, 0

    def enter(self, i, per):
        self.base += self.k
        self.i, self.per, self.k = i, per, 0

    def leave(self, trips):
        assert self.k == self.per, (self.k, self.per)
        self.base += trips * self.per
        self.i, self.per, self.k = 0, 0, 0

    def link(self, ins):
        self.k += 1
        ins.then_inc(self.sem, 1)
        self.eng.wait_ge(self.sem, self.i * self.per + (self.base + self.k))


def build(nc, xT, ctxT, params, heads_row, ssm_cols, dskip, stream, dt_w, c_f32, c_bf, out):
    with ExitStack() as ctx:
        def sb(name, shape, dt=F32):
            return ctx.enter_context(nc.sbuf_tensor(name, shape, dt))

        def sem(name):
            return ctx.enter_context(nc.semaphore(name))

        raw = sb("raw", [P, SLOTS, CHUNK_K * WCOL])
        w_hi = sb("w_hi", [P, SLOTS, CHUNK_K * WCOL], F16)
        w_lo = sb("w_lo", [P, SLOTS, CHUNK_K * WCOL], F16)
        x_res = sb("x_res", [P, KT * TOK])
        ctx_res = sb("ctx_res", [P, KT * TOK])
        norm_hl = sb("norm_hl", [P, 2 * KT * 512], F16)
        mix_hl = sb("mix_hl", [P, 2 * KT * 512], F16)
        stage = sb("stage", [P, KT * TOK])
        tmp = sb("tmp", [P, 4096])
        par = sb("par", [P, N_PCOLS])
        lg_raw = sb("lg_raw", [P, 32])
        lg, lg256, lg_neg = sb("lg", [P, 32]), sb("lg256", [P, 32]), sb("lg_neg", [P, 32])
        hcol = sb("hcol", [SSM_HEADS, 4])
        modraw = sb("modraw", [P, 2 * 48 * 2])
        affine = sb("affine", [P, 2, KT, 2])
        gates = sb("gates", [P, 2 * KT * 2])
        cvec = sb("cvec", [P, KT, 2, 2], F16)
        rstd = sb("rstd", [P, 512])
        eps = sb("eps", [P, 1])
        cst = sb("cst", [P, 896])
        cbf = sb("cbf", [P, 2816], BF16)
        dsk = sb("dsk", [P, KT])

        ident, ones, rot = cst[:, 0:128], cst[:, 128:256], cst[:, 256:384]
        cos, sin = cst[:, 384:640], cst[:, 640:896]
        diff, is_ge, dpos, dneg, is_le = (cbf[:, 512 * n:512 * n + 512] for n in range(5))
        ident_bf, causal_bf = cbf[:, 2560:2688], cbf[:, 2688:2816]

        x3 = x_res[:, :].rearrange("p (t n) -> p t n", t=KT)
        ctx3 = ctx_res[:, :].rearrange("p (t n) -> p t n", t=KT)
        stage16 = stage[:, :].rearrange("p (t n) -> p t n", t=KT)
        stage8 = stage[:, :].rearrange("p (t n) -> p t n", t=8)
        norm_half = [norm_hl[:, h * 8192:(h + 1) * 8192] for h in range(2)]
        mix_half = [mix_hl[:, h * 8192:(h + 1) * 8192] for h in range(2)]
        norm_op = [a.rearrange("p (t n) -> p t n", t=KT) for a in norm_half]
        mix_op = [a.rearrange("p (t n) -> p t n", t=KT) for a in mix_half]
        mix2_op = [a.rearrange("p (t n) -> p t n", t=2 * KT) for a in mix_half]
        hid_op = [a[:, :].rearrange("p (t n) -> p t n", t=64) for a in (norm_hl, mix_hl)]
        u_half = ctx_res[:, :].bitcast(F16)
        u_op = [u_half[:, h * 4096:(h + 1) * 4096].rearrange("p (t n) -> p t n", t=KT) for h in range(2)]
        squares = mix_hl[:, :].bitcast(F32)
        sq512 = squares.rearrange("p (t n) -> p t n", t=KT)

        proj = ctx.enter_context(nc.psum_tensor("proj", [P, 4, 512], F32))
        aux = ctx.enter_context(nc.psum_tensor("aux", [P, 4, 512], F32))

        params_in, x_in, ctx_in = sem("params_in"), sem("x_in"), sem("ctx_in")
        raw_in = [sem(f"raw_in{s}") for s in range(SLOTS)]
        hi_ready, lo_ready = sem("hi_ready"), sem("lo_ready")
        split_free = sem("split_free")
        bank_free = [sem("bank_free_even"), sem("bank_free_odd")]
        act_chain, dve_chain = sem("act_chain"), sem("dve_chain")
        out_done, att_in, dtw_in, heads_in = sem("out_done"), sem("att_in"), sem("dtw_in"), sem("heads_in")
        names = """c_sigmoid c_silu c_hi c_lo lg_ready pads_zero
            squares_ready stat_done rstd_ready scaled norm_hi norm_ready res_done mods_read
            conv_h conv_in conv_y conv_sq conv_sum conv_z conv_g conv_scaled conv_hi conv_done
            kqv_ready rot_done roped vt_psum vt_ready z_sigmoid z_silu mask_exp scores_done p_ready o_psum o_ready
            mean_psum centered osq_ready var_psum orstd_ready y_ready y_hi ret_done
            dtw_hi dtw_lo dt_psum dt_log dt_ready dt_psum_t dt_t cum_psum cum_ready tri_ready
            att_qkv att_vt_psum att_vt att_scores att_max att_exp att_p att_pt_psum att_pt att_o att_hi att_done
            zs_sigmoid zs_ready xbc_pad xbc_conv xbc_sigmoid xbc_ready xt_psum xt_ready gram_psum row_ready
            row_psum decay_ready pw_ready pw_used ssd_psum yg_ready yg_sq yg_psum yg_rstd yg_norm yg_hi ssd_done
            stage_ready relu_ready hid_hi hid_ready""".split()
        sig = {n: sem(n) for n in names}
        LAYERS = [dict(n=512, conv="conv0", ret="ret0", out="out0", conv_order="hcMMbzMM", ret_order="kqMMvzMM"),
                  dict(n=256, conv="conv1", ret="ret1", out="out1", conv_order="hcbz", ret_order="kqvz")]

        def banks(half, n):
            return proj[:, 2 * half:2 * half + 2, 0:n]

        def pair(buf, at, n):
            return buf[:, at:at + 2 * n].rearrange("p (m n) -> p m n", m=2)

        def col(name, k=0):
            return par[:, PCOLS[name] + k:PCOLS[name] + k + 1]

        def cols(name, i, per, k):
            return par[:, bass.ds(i * per + (PCOLS[name] + k), 1)]

        za, zb = mix_hl[:, 4096:8192].bitcast(F32), mix_hl[:, 12288:16384].bitcast(F32)
        pad = tmp[:, 0:1032].rearrange("p (m s n) -> p m s n", m=2, s=2)
        conv_t = tmp[:, 1032:2056]
        conv_sum = tmp[:, 2056:2568]
        conv_sq = tmp[:, 2568:3592]

        k_b, q_b, vt_b, z_b = (stage[:, 1024 * n:1024 * n + 1024] for n in range(4))
        v_b, e_b, s_b = tmp[:, 0:1024], tmp[:, 1024:2048], tmp[:, 2048:3072]
        p_b = tmp[:, 0:1536].rearrange("p (a n) -> p a n", a=3)
        mask_x, mask_c, o_b, t1, t2 = (tmp[:, n:n + 512] for n in (1536, 2048, 2560, 3072, 3584))

        aux2_consts = cbf[:, 512:2560].bitcast(F32)
        acs = aux2_consts[0:SSM_HEADS, 0:384]
        dt_t = aux2_consts[:, 384:448]
        neg_acs = aux2_consts[:, 448:512]
        tri = aux2_consts[:, 512:1024]
        att_log = cst[:, 256:640]
        dtw_hi, dtw_lo = (tmp[:, n:n + 256].bitcast(F16) for n in (512, 768))
        dt_x, dt_e, dt_l, dt_um, dt_eq, dt_a = (tmp[0:SSM_HEADS, n:n + 256] for n in range(1024, 2560, 256))
        adt_t = tmp[:, 2560:2624]
        is_ge_copy = is_ge

        att_qkv = [stage[:, n:n + 512] for n in (0, 512, 1024)]
        att_vt = stage[:, 1536:2048]
        att_s, att_pt = tmp[:, 0:384], tmp[:, 384:768]
        att_m, att_sum, att_r = (tmp[:, n:n + 2] for n in (768, 770, 772))

        zs, zs_e, zs_s = (pair(stage, n, TOK) for n in (0, 512, 1024))
        pad2 = stage[:, 1536:2576].rearrange("p (m n) -> p m n", m=4)
        xt = stage[:, 2576:3088]
        decay_w = stage[:, 3088:3472]
        xbc, xbc_e, xbc_s = (tmp[:, n:n + 1024].rearrange("p (m n) -> p m n", m=4) for n in (0, 1024, 2048))
        rows, pw = tmp[0:SSM_HEADS, 3072:3456], tmp[:, 3456:3840]
        yg, yg_sq = pair(tmp, 1024, TOK), pair(tmp, 1536, TOK)
        c_silu = tmp[:, 64:96].rearrange("p (s t) -> p t s", s=2)

        block = ctx.enter_context(nc.Block())

        @block.sync
        def _(sp):
            sp.dma_start(par[:, :], params).then_inc(params_in, 16)
            sp.dma_start(lg_raw[:, :], heads_row.partition_broadcast(P)).then_inc(heads_in, 16)
            sp.dma_start(x_res[:, :], xT).then_inc(x_in, 16)
            sp.dma_start(ctx_res[:, :], ctxT).then_inc(ctx_in, 16)
            for s in range(SLOTS):
                sp.dma_start(raw[:, s, :], stream[s, :, :]).then_inc(raw_in[s], 16)
            with sp.Fori(1, N_CHUNKS // SLOTS) as i:
                for s in range(SLOTS):
                    sp.wait_ge(lo_ready, i * SLOTS + (s + 1 - SLOTS))
                    sp.dma_start(raw[:, s, :], stream[bass.ds(i * SLOTS + s, 1), :, :].rearrange("a p n -> (a p) n"))\
                      .then_inc(raw_in[s], 16)
            sp.wait_ge(sig["res_done"], RES["mlp"])
            sp.dma_start(out, x_res[:, :]).then_inc(out_done, 16)
            sp.wait_ge(out_done, 16)

        @block.scalar
        def _(act):
            chain = Chain(act, act_chain)
            link = chain.link
            S = sig

            def split_hi(i, per, k):
                for c in range(2):
                    slot = 2 * (k % 2) + c
                    act.wait_ge(raw_in[slot], i * (8 * per) + 16 * (k // 2 + 1))
                    act.wait_ge(split_free, i * (2 * per) + (2 * k + c + 1))
                    act.activation(w_hi[:, slot, :], raw[:, slot, :], ACT.Copy, scale=W_SCALE).then_inc(hi_ready, 1)

            def group_wait(i, per, u):
                act.wait_ge(split_free, i * (2 * per) + (2 * (u + 1) + SLOTS))

            def sigmoid_parts(z, e, s):
                link(act.activation(e, z, ACT.Abs))
                link(act.activation(e, e, ACT.Exp, scale=-1.0))
                link(act.activation(s, e, ACT.Ln, bias=1.0))
                return act.activation(s, s, ACT.Exp, scale=-1.0)

            n_stat, n_hi = [0], [0]

            def make_rstd(n, count):
                n_stat[0] += 1
                act.wait_ge(S["stat_done"], n_stat[0])
                link(act.activation(rstd[:, 0:n], aux[:, 0, 0:n], ACT.Ln, bias=eps[:, :], scale=1.0 / count))
                act.activation(rstd[:, 0:n], rstd[:, 0:n], ACT.Exp, scale=-0.5).then_inc(S["rstd_ready"], 1)

            def square_of(*parts):
                for j, part in enumerate(parts):
                    act.activation(sq512[:, :, j * TOK:(j + 1) * TOK], part, ACT.Square)\
                       .then_inc(S["squares_ready"], 1)

            def norm_hi(dst):
                n_hi[0] += 1
                act.wait_ge(S["scaled"], n_hi[0])
                act.activation(dst, stage16, ACT.Copy).then_inc(S["norm_hi"], 1)

            act.dma_start(cst[:, :], c_f32[:, 0:896]).then_inc(params_in, 16)
            act.dma_start(cbf[:, :], c_bf).then_inc(params_in, 16)
            act.dma_start(dsk[:, :], dskip).then_inc(params_in, 16)
            act.dma_start(hcol[:, 0:2], ssm_cols).then_inc(params_in, 16)
            act.sem_inc(S["decay_ready"], 1)
            act.preload_act_table_set("natural_log_exp_and_others")
            act.wait_ge(params_in, 80)
            sigmoid_parts(par[:, PCOLS["c"]:PCOLS["c"] + 32], tmp[:, 0:32], tmp[:, 32:64]).then_inc(S["c_sigmoid"], 1)
            act.wait_ge(heads_in, 16)
            link(act.activation(lg[:, :], lg_raw[:, :], ACT.Exp))
            link(act.activation(lg[:, :], lg[:, :], ACT.Copy, scale=-1.0))
            link(act.activation(lg256[:, :], lg[:, :], ACT.Copy, scale=float(TOK)))
            link(act.activation(lg_neg[:, :], lg[:, :], ACT.Copy, scale=-1.0))
            split_hi(0, 0, 0)
            act.wait_ge(S["c_silu"], 1)
            act.activation(cvec[:, :, :, 0], c_silu, ACT.Copy, scale=A_SCALE).then_inc(S["c_hi"], 1)

            with act.Fori(0, 8) as i:
                for k in range(2):
                    split_hi(i, 2, k + 1)

            for layer, L in enumerate(LAYERS):
                n, r0 = L["n"], 4 * layer
                if layer == 0:
                    act.wait_ge(x_in, 16)
                    act.wait_ge(ctx_in, 16)
                else:
                    act.wait_ge(S["res_done"], RES["out0"])
                square_of(x3, ctx3)
                make_rstd(512, D)
                norm_hi(norm_op[0][:, :, 0:TOK])
                norm_hi(norm_op[0][:, :, TOK:512])

                order = L["conv_order"]
                per, u0, g0 = len(order), U0[L["conv"]], G0[L["conv"]]
                h_t, z_t = pair(za, 0, 512)[:, :, 0:n], pair(za, 1024, 512)[:, :, 0:n]
                e_t, s_t = pair(zb, 0, 512)[:, :, 0:n], pair(zb, 1024, 512)[:, :, 0:n]
                sq_t = pair(conv_sq, 0, 512)[:, :, 0:n]
                with act.Fori(0, 4) as i:
                    chain.enter(i, 4)
                    for k, what in enumerate(order):
                        split_hi(i, per, u0 + k + 1)
                        if what == "h":
                            group_wait(i, per, u0 + k)
                            act.wait_ge(S["conv_in"], i + r0 + 1)
                            link(act.activation(h_t, banks(k % 2, n), ACT.Copy, scale=UNSCALE))
                            act.sem_inc(S["conv_h"], 1)
                            act.sem_inc(bank_free[k % 2], 1)
                        if what == "z":
                            act.wait_ge(S["conv_y"], i + (r0 + 1))
                            act.wait_ge(S["conv_sum"], i + r0 + 1)
                            act.activation(sq_t, stage8[:, bass.ds(i * 2, 2), 0:n], ACT.Square)\
                               .then_inc(S["conv_sq"], 1)
                            group_wait(i, per, u0 + k)
                            act.wait_ge(S["conv_g"], i + r0 + 1)
                            act.activation(z_t, banks(k % 2, n), ACT.Copy, scale=UNSCALE)\
                               .then_inc(bank_free[k % 2], 1)
                            act.wait_ge(bank_free[k % 2], i * (per // 2) + ((g0 + k) // 2 + 2))
                            sigmoid_parts(z_t, e_t, s_t).then_inc(S["conv_z"], 1)
                chain.leave(4)
                make_rstd(n, D // 2)
                act.wait_ge(S["conv_scaled"], layer + 1)
                act.activation(mix_op[0][:, 0:8, 0:n], stage8[:, :, 0:n], ACT.Copy, scale=A_SCALE)\
                   .then_inc(S["conv_hi"], 1)

                order = L["ret_order"]
                per, u0, g0 = len(order), U0[L["ret"]], G0[L["ret"]]
                act.wait_ge(S["conv_done"], layer + 1)
                with act.Fori(0, 4) as i:
                    chain.enter(i, 3 + 2 * 2)
                    for k, what in enumerate(order):
                        split_hi(i, per, u0 + k + 1)
                        if what == "M":
                            continue
                        group_wait(i, per, u0 + k)
                        if what in "kqv":
                            m = 512 if what != "q" else n
                            dst = {"k": k_b, "q": q_b, "v": v_b}[what]
                            if what == "k":
                                act.wait_ge(S["ret_done"], i * 2 + 2 * r0 + 1)
                            act.activation(pair(dst, 0, 512)[:, :, 0:m], banks(k % 2, m), ACT.Copy,
                                           scale=UNSCALE * (HEAD_SCALE if what == "k" else 1.0))\
                               .then_inc(S["kqv_ready"], 1)
                            act.wait_ge(S["kqv_ready"], i * 3 + (3 * r0 + "kqv".index(what) + 1))
                            act.sem_inc(bank_free[k % 2], 1)
                        else:
                            z_t, e_t, s_t = (pair(b, 0, 512)[:, :, 0:n] for b in (z_b, e_b, s_b))
                            act.activation(z_t, banks(k % 2, n), ACT.Copy, scale=UNSCALE).then_inc(bank_free[k % 2], 1)
                            act.wait_ge(bank_free[k % 2], i * (per // 2) + ((g0 + k) // 2 + 2))
                            act.wait_ge(S["roped"], i * 2 + (2 * r0 + 2))
                            sigmoid_parts(z_t, e_t, s_t).then_inc(S["z_sigmoid"], 1)
                    act.wait_ge(S["vt_psum"], i + (r0 + 1))
                    act.activation(vt_b[:, :], aux[:, 2:4, :], ACT.Copy).then_inc(S["vt_ready"], 1)
                    act.wait_ge(S["z_silu"], i + (r0 + 1))
                    for h in range(2):
                        lgf = lg[:, bass.ds(i * 2 + (layer * 8 + h), 1)]
                        lgb = lg[:, bass.ds(i * 2 + (16 + layer * 8 + h), 1)]
                        lgb_neg = lg_neg[:, bass.ds(i * 2 + (16 + layer * 8 + h), 1)]
                        lgf256 = lg256[:, bass.ds(i * 2 + (layer * 8 + h), 1)]
                        lgb256 = lg256[:, bass.ds(i * 2 + (16 + layer * 8 + h), 1)]
                        if h:
                            act.wait_ge(S["ret_done"], i * 2 + (2 * r0 + h) + 1)
                        act.activation(mask_x, dpos, ACT.Exp, scale=lgf).then_inc(S["mask_exp"], 1)
                        act.activation(t1, dneg, ACT.Exp, scale=lgb).then_inc(S["mask_exp"], 1)
                        act.activation(mask_c, diff, ACT.Exp, scale=lgf, bias=lgf256).then_inc(S["mask_exp"], 1)
                        act.activation(t2, diff, ACT.Exp, scale=lgb_neg, bias=lgb256).then_inc(S["mask_exp"], 1)
                        hd = i * 2 + (2 * r0 + h + 1)
                        act.wait_ge(S["o_psum"], hd)
                        act.activation(o_b[:, 0:n], aux[:, 3, 0:n], ACT.Copy).then_inc(S["o_ready"], 1)
                        act.wait_ge(S["centered"], hd)
                        act.activation(t1[:, 0:n], o_b[:, 0:n], ACT.Square).then_inc(S["osq_ready"], 1)
                        act.wait_ge(S["var_psum"], hd)
                        link(act.activation(rstd[:, 0:n], aux[:, 1, 0:n], ACT.Ln, bias=eps[:, :], scale=1.0 / P))
                        act.activation(rstd[:, 0:n], rstd[:, 0:n], ACT.Exp, scale=-0.5).then_inc(S["orstd_ready"], 1)
                        act.wait_ge(S["y_ready"], hd)
                        link(act.activation(mix_op[0][:, bass.ds(i * 2 + (8 + h), 1), 0:n],
                                            o_b[:, 0:n].rearrange("p (a n) -> p a n", a=1), ACT.Copy, scale=A_SCALE))
                        act.sem_inc(S["y_hi"], 1)
                chain.leave(4)

                u0 = U0[L["out"]]
                with act.Fori(0, 4) as i:
                    for k in range(2):
                        split_hi(i, 2, u0 + k + 1)

            act.wait_ge(S["res_done"], RES["out1"])
            act.dma_start(att_log, c_f32[:, 896:1280]).then_inc(att_in, 16)
            act.dma_start(tmp[:, 0:512], dt_w).then_inc(dtw_in, 16)
            square_of(x3)
            make_rstd(TOK, D)
            act.wait_ge(S["res_done"], RES["final"])
            square_of(x3)
            make_rstd(TOK, D)
            norm_hi(u_op[0])

            act.wait_ge(dtw_in, 16)
            act.activation(dtw_hi, tmp[:, 0:512], ACT.Copy, scale=W_SCALE).then_inc(S["dtw_hi"], 1)
            act.activation(tri, is_ge_copy, ACT.Copy).then_inc(S["tri_ready"], 1)
            act.wait_ge(S["dt_psum"], 1)
            link(act.activation(dt_x, aux[0:32, 1, 0:TOK], ACT.Identity, scale=UNSCALE, bias=hcol[:, 0:1]))
            link(act.activation(dt_e, dt_x, ACT.Abs))
            link(act.activation(dt_e, dt_e, ACT.Exp, scale=-1.0))
            link(act.activation(hcol[:, 2:3], hcol[:, 1:2], ACT.Exp))
            act.activation(dt_l, dt_e, ACT.Ln, bias=1.0).then_inc(S["dt_log"], 1)
            act.wait_ge(S["dt_psum_t"], 1)
            act.activation(dt_t, aux[:, 2, 0:64], ACT.Copy).then_inc(S["dt_t"], 1)
            act.activation(adt_t, aux[:, 2, 64:128], ACT.Copy).then_inc(S["dt_t"], 1)
            act.wait_ge(S["cum_psum"], 1)
            act.activation(acs[:, 0:256], aux[0:32, 3, 0:256], ACT.Copy).then_inc(S["cum_ready"], 1)
            act.activation(acs[:, 256:384], aux[0:32, 3, 128:256], ACT.Copy).then_inc(S["cum_ready"], 1)
            act.activation(neg_acs, aux[:, 3, 256:320], ACT.Copy, scale=-1.0).then_inc(S["cum_ready"], 1)

            u0, g0 = U0["att"], G0["att"]
            with act.Fori(0, 4) as i:
                for k in range(6):
                    split_hi(i, 6, u0 + k + 1)
                    sub, what = k // 3, k % 3
                    group_wait(i, 6, u0 + k)
                    if what == 0:
                        act.wait_ge(S["att_done"], i * 4 + 2 * sub + 1)
                    act.activation(pair(att_qkv[what], 0, TOK), banks(k % 2, TOK), ACT.Copy,
                                   scale=UNSCALE * (HEAD_SCALE if what == 0 else 1.0)).then_inc(S["att_qkv"], 1)
                    act.wait_ge(S["att_qkv"], i * 6 + (k + 1))
                    act.sem_inc(bank_free[k % 2], 1)
                    if what < 2:
                        continue
                    act.wait_ge(S["att_vt_psum"], i * 2 + (sub + 1))
                    act.activation(att_vt, aux[:, 2, :], ACT.Copy).then_inc(S["att_vt"], 1)
                    for m in range(2):
                        hd = i * 4 + (2 * sub + m + 1)
                        act.wait_ge(S["att_max"], hd)
                        act.activation(att_s[:, 0:128], att_s[:, 0:128], ACT.Exp, bias=att_m[:, 0:1],
                                       accum_out=att_sum[:, 0:1]).then_inc(S["att_exp"], 1)
                        act.activation(att_s[:, 128:384], att_s[:, 128:384], ACT.Exp, bias=att_m[:, 1:2],
                                       accum_out=att_sum[:, 1:2]).then_inc(S["att_exp"], 1)
                        act.wait_ge(S["att_pt_psum"], hd)
                        act.activation(att_pt, aux[:, 1, 0:384], ACT.Copy).then_inc(S["att_pt"], 1)
                        act.wait_ge(S["att_o"], hd)
                        act.activation(mix2_op[0][:, bass.ds(i * 4 + (KT + 2 * sub + m), 1), :],
                                       aux[:, 3:4, 0:TOK], ACT.Copy, scale=A_SCALE).then_inc(S["att_hi"], 1)

            u0, g0 = U0["ssd"], G0["ssd"]
            with act.Fori(0, 4) as i:
                chain.enter(i, 2 * (3 + 2 * 3 + 1))
                for k in range(6):
                    split_hi(i, 6, u0 + k + 1)
                    sub, what = k // 3, k % 3
                    group_wait(i, 6, u0 + k)
                    if what == 0:
                        act.wait_ge(S["ssd_done"], i * 2 + sub + 1)
                        act.activation(zs, banks(k % 2, TOK), ACT.Copy, scale=UNSCALE).then_inc(bank_free[k % 2], 1)
                        act.wait_ge(bank_free[k % 2], i * 3 + ((g0 + k) // 2 + 2))
                        sigmoid_parts(zs, zs_e, zs_s).then_inc(S["zs_sigmoid"], 1)
                    else:
                        q = what - 1
                        act.activation(pad2[:, 2 * q:2 * q + 2, 3:3 + TOK], banks(k % 2, TOK), ACT.Copy, scale=UNSCALE)\
                           .then_inc(S["xbc_pad"], 1)
                        act.wait_ge(S["xbc_pad"], i * 4 + (2 * sub + q + 1))
                        act.sem_inc(bank_free[k % 2], 1)
                        act.wait_ge(S["xbc_conv"], i * 4 + (2 * sub + q + 1))
                        sigmoid_parts(xbc[:, 2 * q:2 * q + 2, :], xbc_e[:, 2 * q:2 * q + 2, :],
                                      xbc_s[:, 2 * q:2 * q + 2, :]).then_inc(S["xbc_sigmoid"], 1)
                    if what < 2:
                        continue
                    act.wait_ge(S["xt_psum"], i * 2 + (sub + 1))
                    act.activation(xt, aux[:, 0, :], ACT.Copy).then_inc(S["xt_ready"], 1)
                    for r in range(4):
                        act.wait_ge(S["row_psum"], i * 8 + (4 * sub + r + 1) + 1)
                        act.wait_ge(S["pw_ready"], i * 8 + (4 * sub + r) + 1)
                        act.activation(decay_w[:, 0:256], aux[:, 2, 0:256], ACT.Exp,
                                       bias=neg_acs[:, bass.ds(i * 8 + (4 * sub + r), 1)]).then_inc(S["decay_ready"], 1)
                        act.activation(decay_w[:, 256:384], aux[:, 2, 256:384], ACT.Exp,
                                       bias=neg_acs[:, bass.ds(i * 8 + (32 + 4 * sub + r), 1)])\
                           .then_inc(S["decay_ready"], 1)
                    gr = i * 2 + (sub + 1)
                    act.wait_ge(S["yg_ready"], gr)
                    act.activation(yg_sq, yg, ACT.Square).then_inc(S["yg_sq"], 1)
                    act.wait_ge(S["yg_psum"], gr)
                    link(act.activation(rstd[:, 0:TOK], aux[:, 0, 0:TOK], ACT.Ln, bias=eps[:, :], scale=1.0 / 256))
                    act.activation(rstd[:, 0:TOK], rstd[:, 0:TOK], ACT.Exp, scale=-0.5).then_inc(S["yg_rstd"], 1)
                    act.wait_ge(S["yg_norm"], gr)
                    act.activation(mix2_op[0][:, bass.ds(i * 4 + 2 * sub, 2), :], yg, ACT.Copy, scale=A_SCALE)\
                       .then_inc(S["yg_hi"], 1)
            chain.leave(4)

            def collect(phase, units, first, last_unit):
                def body(i, tail):
                    for k in range(2):
                        for w in range(units):
                            if not (tail and k == 1 and w == units - 1):
                                split_hi(i, 2 * units, U0[phase] + units * k + w + 1)
                        group_wait(i, 2 * units, U0[phase] + units * k + units - 1)
                        act.activation(stage16[:, bass.ds(i * 4 + 2 * k, 2), :], banks(k, TOK), ACT.Copy, scale=UNSCALE)\
                           .then_inc(S["stage_ready"], 1)
                        act.wait_ge(S["stage_ready"], i * 2 + (first + k + 1))
                        act.sem_inc(bank_free[k], 1)
                with act.Fori(0, 3 if last_unit else 4) as i:
                    body(i, False)
                if last_unit:
                    body(3, True)

            act.wait_ge(S["ssd_done"], SSM_GROUPS + 1)
            collect("mixout", 2, 0, False)
            square_of(stage16)
            make_rstd(TOK, D)
            act.wait_ge(S["res_done"], RES["mix"])
            square_of(x3)
            make_rstd(TOK, D)
            norm_hi(u_op[0])

            with act.Fori(0, 16) as i:
                for k in range(2):
                    split_hi(i, 2, U0["up"] + k + 1)
                    act.wait_ge(S["relu_ready"], i * 2 + (k + 1))
                    hid_t = pair(tmp, 1024 + 512 * k, TOK)
                    act.activation(hid_t, pair(tmp, 512 * k, TOK), ACT.Square, scale=A_SCALE ** 0.5)\
                       .then_inc(S["hid_hi"], 1)
                    act.wait_ge(S["hid_hi"], i * 4 + (2 * k + 1))
                    act.activation(hid_op[0][:, bass.ds(i * 4 + 2 * k, 2), :], hid_t, ACT.Copy)\
                       .then_inc(S["hid_hi"], 1)
            collect("down", 4, 8, True)
            square_of(stage16)
            make_rstd(TOK, D)

        @block.tensor
        def _(pe):
            S = sig

            def unit(i, per, k, n, op, kt0, half, first, last):
                for c in range(2):
                    slot = 2 * (k % 2) + c
                    pe.wait_ge(lo_ready, i * (2 * per) + (2 * k + c + 1))
                    for t in range(CHUNK_K):
                        kt = kt0 + CHUNK_K * c + t
                        for m in range(2):
                            acc = proj[:, 2 * half + m, 0:n]
                            hi = w_hi[:, slot, t * WCOL + m * P:t * WCOL + (m + 1) * P]
                            lo = w_lo[:, slot, t * WCOL + m * P:t * WCOL + (m + 1) * P]
                            begin, end = first and c == 0 and t == 0, last and c == 1 and t == CHUNK_K - 1
                            pe.matmul(acc, hi, op[0][:, kt, 0:n], start=begin, stop=False)
                            pe.matmul(acc, hi, op[1][:, kt, 0:n], start=False, stop=False)
                            mm = pe.matmul(acc, lo, op[0][:, kt, 0:n], start=False, stop=end)
                    mm.then_inc(split_free, 1)
                return mm

            def mod_unit(i, per, k, half):
                for c in range(2):
                    slot = 2 * (k % 2) + c
                    pe.wait_ge(lo_ready, i * (2 * per) + (2 * k + c + 1))
                    for t in range(CHUNK_K):
                        kt = CHUNK_K * c + t
                        vec = cvec[:, kt, :, :].rearrange("p s h -> p (s h)")
                        for m in range(2):
                            acc = proj[:, 2 * half + m, 0:4]
                            for w in (w_hi, w_lo):
                                mm = pe.matmul(acc, w[:, slot, t * WCOL + m * P:t * WCOL + (m + 1) * P], vec,
                                               start=kt == 0 and w is w_hi, stop=kt == KT - 1 and w is w_lo)
                    mm.then_inc(split_free, 1)

            def bank_wait(i, per, g):
                pe.wait_ge(bank_free[g % 2], i * (per // 2) + (g // 2 + 1))

            n_stat, n_sq = [0], [0]

            def stat(n, parts):
                n_sq[0] += parts
                n_stat[0] += 1
                pe.wait_ge(S["squares_ready"], n_sq[0])
                for t in range(KT):
                    mm = pe.matmul(aux[:, 0, 0:n], ones, sq512[:, t, 0:n], start=t == 0, stop=t == KT - 1)
                mm.then_inc(S["stat_done"], 1)

            for name in ("row_psum", "pw_used"):
                pe.sem_inc(S[name], 1)
            pe.sem_inc(split_free, SLOTS)
            pe.sem_inc(bank_free[0], 1)
            pe.sem_inc(bank_free[1], 1)
            pe.wait_ge(params_in, 80)
            pe.wait_ge(S["c_lo"], 1)
            with pe.Fori(0, 8) as i:
                for k in range(2):
                    bank_wait(i, 2, k)
                    mod_unit(i, 2, k, k)

            n_norm = [0]

            def norm_wait(parts):
                n_norm[0] += parts
                pe.wait_ge(S["norm_ready"], n_norm[0])

            for layer, L in enumerate(LAYERS):
                n, r0 = L["n"], 4 * layer
                stat(512, 2)
                norm_wait(2)

                order = L["conv_order"]
                per, u0, g0 = len(order), U0[L["conv"]], G0[L["conv"]]
                with pe.Fori(0, 4) as i:
                    for k, what in enumerate(order):
                        bank_wait(i, per, g0 + k)
                        if what == "M":
                            mod_unit(i, per, u0 + k, k % 2)
                        else:
                            unit(i, per, u0 + k, n, norm_op, 0, k % 2, True, True)
                n_stat[0] += 1
                pe.wait_ge(S["conv_sum"], r0 + 4 + 1)
                pe.matmul(aux[:, 0, 0:n], ones, conv_sum[:, 0:n], start=True, stop=True).then_inc(S["stat_done"], 1)

                order = L["ret_order"]
                per, u0, g0 = len(order), U0[L["ret"]], G0[L["ret"]]
                pe.wait_ge(S["rstd_ready"], n_stat[0])
                with pe.Fori(0, 4) as i:
                    for k, what in enumerate(order):
                        bank_wait(i, per, g0 + k)
                        if what == "M":
                            mod_unit(i, per, u0 + k, k % 2)
                            continue
                        m = n if what in "qz" else 512
                        unit(i, per, u0 + k, m, norm_op, 0, k % 2, True, True)
                        if what == "q":
                            pe.wait_ge(S["kqv_ready"], i * 3 + (3 * r0 + 1))
                            pe.matmul(aux[:, 0, :], rot, pair(k_b, 0, 512)[:, :, 0:TOK], start=True, stop=True)\
                              .then_inc(S["rot_done"], 1)
                        if what == "v":
                            pe.wait_ge(S["kqv_ready"], i * 3 + (3 * r0 + 2))
                            pe.matmul(aux[:, 1, :], rot, pair(q_b, 0, 512)[:, :, 0:TOK], start=True, stop=True)\
                              .then_inc(S["rot_done"], 1)
                    pe.wait_ge(S["kqv_ready"], i * 3 + (3 * r0 + 3))
                    for h in range(2):
                        for j in range(4):
                            mm = pe.transpose(aux[:, 2 + h, j * P:(j + 1) * P],
                                              v_b[:, h * 512 + j * P:h * 512 + (j + 1) * P], ident)
                    mm.then_inc(S["vt_psum"], 1)
                    pe.wait_ge(S["roped"], i * 2 + (2 * r0 + 2))
                    pe.wait_ge(S["vt_ready"], i + (r0 + 1))
                    for h in range(2):
                        hd = i * 2 + (2 * r0 + h + 1)
                        kk, qq = k_b[:, h * 512:(h + 1) * 512], q_b[:, h * 512:(h + 1) * 512]
                        if h:
                            pe.wait_ge(S["ret_done"], i * 2 + (2 * r0 + h) + 1)
                        for j in range(2):
                            mm = pe.matmul(aux[:, 0, j * TOK:(j + 1) * TOK], kk[:, j * P:(j + 1) * P], qq[:, 0:TOK],
                                           start=True, stop=True)
                        for j in range(2):
                            ck = kk[:, TOK + j * P:TOK + (j + 1) * P]
                            mm = pe.matmul(aux[:, 1, j * TOK:(j + 1) * TOK], ck, qq[:, 0:TOK], start=True, stop=True)
                            if n == 512:
                                mm = pe.matmul(aux[:, 2, j * TOK:(j + 1) * TOK], ck, qq[:, TOK:512],
                                               start=True, stop=True)
                        mm.then_inc(S["scores_done"], 1)
                        pe.wait_ge(S["p_ready"], hd)
                        vt = [vt_b[:, h * 512 + j * P:h * 512 + (j + 1) * P] for j in range(4)]
                        for j in range(4):
                            mm = pe.matmul(aux[:, 3, 0:TOK], vt[j], p_b[:, j // 2, (j % 2) * TOK:(j % 2 + 1) * TOK],
                                           start=j == 0, stop=j == 3)
                        if n == 512:
                            for j in range(2):
                                mm = pe.matmul(aux[:, 3, TOK:512], vt[2 + j], p_b[:, 2, j * TOK:(j + 1) * TOK],
                                               start=j == 0, stop=j == 1)
                        mm.then_inc(S["o_psum"], 1)
                        pe.wait_ge(S["o_ready"], hd)
                        pe.matmul(aux[:, 0, 0:n], ones, o_b[:, 0:n], start=True, stop=True).then_inc(S["mean_psum"], 1)
                        pe.wait_ge(S["osq_ready"], hd)
                        pe.matmul(aux[:, 1, 0:n], ones, t1[:, 0:n], start=True, stop=True).then_inc(S["var_psum"], 1)

                pe.wait_ge(S["conv_done"], layer + 1)
                pe.wait_ge(S["ret_done"], 8 * (layer + 1) + 1)
                u0, g0 = U0[L["out"]], G0[L["out"]]
                with pe.Fori(0, 4) as i:
                    for k in range(2):
                        bank_wait(i, 2, g0 + k)
                        unit(i, 2, u0 + k, n, mix_op, 0, k, True, True)

            stat(TOK, 1)
            stat(TOK, 1)
            norm_wait(1)

            pe.wait_ge(S["dtw_lo"], 1)
            for t in range(KT):
                wh, wl = (w[:, 32 * t:32 * t + 32] for w in (dtw_hi, dtw_lo))
                pe.matmul(aux[0:32, 1, 0:TOK], wh, u_op[0][:, t, :], start=t == 0, stop=False)
                pe.matmul(aux[0:32, 1, 0:TOK], wh, u_op[1][:, t, :], start=False, stop=False)
                mm = pe.matmul(aux[0:32, 1, 0:TOK], wl, u_op[0][:, t, :], start=False, stop=t == KT - 1)
            mm.then_inc(S["dt_psum"], 1)
            pe.wait_ge(S["dt_ready"], 1)
            for n_, src in enumerate((dt_x, dt_a)):
                for j in range(2):
                    mm = pe.transpose(aux[:, 2, 64 * n_ + 32 * j:64 * n_ + 32 * j + 32], src[:, j * P:(j + 1) * P],
                                      ident[0:32, 0:32])
            mm.then_inc(S["dt_psum_t"], 1)
            pe.wait_ge(S["dt_t"], 2)
            pe.wait_ge(S["tri_ready"], 1)
            for j in range(2):
                pe.matmul(aux[0:32, 3, 0:TOK], adt_t[:, 32 * j:32 * j + 32], tri[:, j * TOK:(j + 1) * TOK],
                          start=j == 0, stop=j == 1)
            for q in range(2):
                for j in range(2):
                    mm = pe.matmul(aux[:, 3, TOK + 32 * q:TOK + 32 * q + 32],
                                   tri[:, j * TOK + q * P:j * TOK + (q + 1) * P], adt_t[:, 32 * j:32 * j + 32],
                                   start=j == 0, stop=j == 1)
            mm.then_inc(S["cum_psum"], 1)
            pe.wait_ge(S["cum_ready"], 3)

            u0, g0 = U0["att"], G0["att"]
            with pe.Fori(0, 4) as i:
                for k in range(6):
                    bank_wait(i, 6, g0 + k)
                    unit(i, 6, u0 + k, TOK, u_op, 0, k % 2, True, True)
                    sub, what = k // 3, k % 3
                    if what < 2:
                        continue
                    pe.wait_ge(S["att_qkv"], i * 6 + (3 * sub + 3))
                    for m in range(2):
                        for j in range(2):
                            mm = pe.transpose(aux[:, 2, m * TOK + j * P:m * TOK + (j + 1) * P],
                                              att_qkv[2][:, m * TOK + j * P:m * TOK + (j + 1) * P], ident)
                    mm.then_inc(S["att_vt_psum"], 1)
                    for m in range(2):
                        hd = i * 4 + (2 * sub + m + 1)
                        q_, k_ = att_qkv[0][:, m * TOK:(m + 1) * TOK], att_qkv[1][:, m * TOK:(m + 1) * TOK]
                        pe.matmul(aux[:, 0, 0:P], q_[:, 0:P], k_[:, 0:P], start=True, stop=True)
                        pe.matmul(aux[:, 0, P:P + TOK], q_[:, P:TOK], k_, start=True, stop=True)\
                          .then_inc(S["att_scores"], 1)
                        pe.wait_ge(S["att_p"], hd)
                        for j in range(3):
                            mm = pe.transpose(aux[:, 1, j * P:(j + 1) * P], att_s[:, j * P:(j + 1) * P], ident)
                        mm.then_inc(S["att_pt_psum"], 1)
                        pe.wait_ge(S["att_vt"], i * 2 + (sub + 1))
                        pe.wait_ge(S["att_pt"], hd)
                        if m == 0:
                            pe.wait_ge(S["att_done"], i * 4 + 2 * sub + 1)
                        else:
                            pe.wait_ge(S["att_done"], i * 4 + (2 * sub + 1) + 1)
                        v0, v1 = (att_vt[:, m * TOK + j * P:m * TOK + (j + 1) * P] for j in range(2))
                        pe.matmul(aux[:, 3, 0:TOK], v0, att_pt[:, 0:TOK], start=True, stop=False)
                        pe.matmul(aux[:, 3, P:TOK], v1, att_pt[:, TOK:384], start=False, stop=True)\
                          .then_inc(S["att_o"], 1)

            u0, g0 = U0["ssd"], G0["ssd"]
            with pe.Fori(0, 4) as i:
                for k in range(6):
                    bank_wait(i, 6, g0 + k)
                    unit(i, 6, u0 + k, TOK, u_op, 0, k % 2, True, True)
                    sub, what = k // 3, k % 3
                    if what < 2:
                        continue
                    pe.wait_ge(S["xbc_ready"], i * 4 + (2 * sub + 2))
                    for m in range(2):
                        for j in range(2):
                            mm = pe.transpose(aux[:, 0, j * TOK + m * P:j * TOK + (m + 1) * P],
                                              xbc[:, m, j * P:(j + 1) * P], ident)
                    mm.then_inc(S["xt_psum"], 1)
                    pe.matmul(aux[:, 1, 0:TOK], xbc[:, 2, 0:P], xbc[:, 3, :], start=True, stop=True)
                    pe.matmul(aux[:, 1, TOK:384], xbc[:, 2, P:TOK], xbc[:, 3, P:TOK], start=True, stop=True)\
                      .then_inc(S["gram_psum"], 1)
                    pe.wait_ge(S["xt_ready"], i * 2 + (sub + 1))

                    def rows_out(r):
                        hd = i * 8 + (4 * sub + r + 1)
                        pe.wait_ge(S["row_ready"], hd)
                        pe.wait_ge(S["decay_ready"], i * 16 + 2 * (4 * sub + r) + 1)
                        pe.matmul(aux[:, 2, 0:384], ones[0:SSM_HEADS, :], rows, start=True, stop=False)
                        pe.matmul(aux[:, 2, 0:P], ident_bf, causal_bf, start=False, stop=False)
                        pe.matmul(aux[:, 2, TOK:384], ident_bf, causal_bf, start=False, stop=True)\
                          .then_inc(S["row_psum"], 1)

                    rows_out(0)
                    for r in range(4):
                        if r < 3:
                            rows_out(r + 1)
                        hd = i * 8 + (4 * sub + r + 1)
                        pe.wait_ge(S["pw_ready"], hd + 1)
                        at, m = (r % 2) * 64, r // 2
                        pe.matmul(aux[at:at + 64, 3, m * TOK:(m + 1) * TOK], xt[:, m * P + at:m * P + at + 64],
                                  pw[:, 0:TOK], start=True, stop=False)
                        pe.matmul(aux[at:at + 64, 3, m * TOK + P:(m + 1) * TOK],
                                  xt[:, TOK + m * P + at:TOK + m * P + at + 64], pw[:, TOK:384],
                                  start=False, stop=True).then_inc(S["pw_used"], 1)
                    pe.wait_ge(S["yg_sq"], i * 2 + (sub + 1))
                    pe.matmul(aux[:, 0, 0:TOK], ones, yg_sq[:, 0, :], start=True, stop=False)
                    pe.matmul(aux[:, 0, 0:TOK], ones, yg_sq[:, 1, :], start=False, stop=True)\
                      .then_inc(S["yg_psum"], 1)

            pe.wait_ge(S["ssd_done"], SSM_GROUPS + 1)
            pe.wait_ge(S["att_done"], ATT_HEADS + 1)
            with pe.Fori(0, 4) as i:
                for k in range(2):
                    bank_wait(i, 2, G0["mixout"] + k)
                    for w in range(2):
                        unit(i, 4, U0["mixout"] + 2 * k + w, TOK, mix2_op, KT * w, k, w == 0, w == 1)
            stat(TOK, 1)
            stat(TOK, 1)
            norm_wait(1)
            with pe.Fori(0, 16) as i:
                for k in range(2):
                    bank_wait(i, 2, G0["up"] + k)
                    unit(i, 2, U0["up"] + k, TOK, u_op, 0, k, True, True)
            pe.wait_ge(S["hid_ready"], 32)
            with pe.Fori(0, 4) as i:
                for k in range(2):
                    bank_wait(i, 2, G0["down"] + k)
                    for w in range(4):
                        unit(i, 8, U0["down"] + 4 * k + w, TOK, hid_op, KT * w, k, w == 0, w == 3)
            stat(TOK, 1)

        @block.vector
        def _(dve):
            chain = Chain(dve, dve_chain)
            link = chain.link
            S = sig
            stt = dve.scalar_tensor_tensor

            def split_lo(i, per, k):
                for c in range(2):
                    slot = 2 * (k % 2) + c
                    dve.wait_ge(hi_ready, i * (2 * per) + (2 * k + c + 1))
                    stt(w_lo[:, slot, :], raw[:, slot, :], W_SCALE, w_hi[:, slot, :], ALU.mult, ALU.subtract)\
                        .then_inc(lo_ready, 1)

            def group_wait(i, per, u):
                dve.wait_ge(split_free, i * (2 * per) + (2 * (u + 1) + SLOTS))

            def silu(z, e, s):
                link(stt(e, z, 0.0, e, ALU.min, ALU.mult))
                link(stt(z, z, 0.0, e, ALU.max, ALU.add))
                return dve.tensor_tensor(z, z, s, ALU.mult)

            def over(v, reps):
                return v.rearrange("p (a n) -> p a n", a=1).to_broadcast([P, reps, v.shape[-1]])

            for name in ("conv_in", "conv_sum", "conv_g", "ret_done", "att_done", "ssd_done", "pw_ready"):
                dve.sem_inc(S[name], 1)
            dve.memset(eps[:, :], EPS).then_inc(dve_chain, 1)
            chain.k += 1
            dve.wait_ge(S["c_sigmoid"], 1)
            cc = par[:, PCOLS["c"]:PCOLS["c"] + 32]
            silu_c = tmp[:, 64:96]
            link(stt(silu_c, cc, 0.0, tmp[:, 0:32], ALU.min, ALU.mult))
            link(stt(silu_c, cc, 0.0, silu_c, ALU.max, ALU.add))
            dve.tensor_tensor(silu_c, silu_c, tmp[:, 32:64], ALU.mult).then_inc(S["c_silu"], 1)
            split_lo(0, 0, 0)
            dve.wait_ge(S["c_silu"], 1)
            dve.wait_ge(S["c_hi"], 1)
            stt(cvec[:, :, :, 1], c_silu, A_SCALE, cvec[:, :, :, 0], ALU.mult, ALU.subtract).then_inc(S["c_lo"], 1)

            def mod_out(i, tiles, tile0, half):
                dst = modraw[:, bass.ds(i * (2 * tiles) + 2 * tile0, 4)].rearrange("p (m s) -> p m s", m=2)
                src = proj[:, 2 * half:2 * half + 2, 0:4].rearrange("p m (s h) -> p m s h", h=2)
                dve.tensor_reduce(dst, src, AX.X, ALU.add).then_inc(bank_free[half], 1)

            with dve.Fori(0, 8) as i:
                for k in range(2):
                    split_lo(i, 2, k + 1)
                    group_wait(i, 2, k)
                    mod_out(i, 4, 2 * k, k)

            def mod_view(layer, t0, t1):
                return modraw[:, 96 * layer + 2 * t0:96 * layer + 2 * t1].rearrange("p (t s) -> p t s", s=2)

            def per_tile(name, t0, t1):
                c0 = PCOLS[name]
                return par[:, c0 + t0:c0 + t1].rearrange("p (t a) -> p t a", a=1).to_broadcast([P, t1 - t0, 2])

            def make_affine(layer):
                m = mod_view(layer, 0, 2 * KT)
                link(stt(m, m, UNSCALE, per_tile("b_mod", 48 * layer, 48 * layer + 2 * KT), ALU.mult, ALU.add))
                link(stt(affine[:, 0, :, :], mod_view(layer, KT, 2 * KT), 1.0,
                         per_tile("norm_w", KT * layer, KT * (layer + 1)), ALU.add, ALU.mult))
                link(dve.tensor_scalar(affine[:, 0, :, :], affine[:, 0, :, :], A_SCALE, None, ALU.mult))
                link(dve.tensor_scalar(affine[:, 1, :, :], mod_view(layer, 0, KT), A_SCALE, None, ALU.mult))

            def make_gates():
                for layer in range(2):
                    g = gates[:, 32 * layer:32 * layer + 32].rearrange("p (t s) -> p t s", s=2)
                    link(stt(g, mod_view(layer, 2 * KT, 3 * KT), UNSCALE,
                             per_tile("b_mod", 48 * layer + 2 * KT, 48 * layer + 3 * KT), ALU.mult, ALU.add))
                    link(dve.tensor_scalar(g, g, UNSCALE, None, ALU.mult))

            n_stat, n_hi, n_norm = [0], [0], [0]

            def rstd_wait():
                n_stat[0] += 1
                dve.wait_ge(S["rstd_ready"], n_stat[0])

            def norm_split(src, s, scale_shift, dst_hi, dst_lo):
                link(dve.tensor_tensor(stage16, src, over(rstd[:, s * TOK:(s + 1) * TOK], KT), ALU.mult))
                for t in range(KT):
                    ins = scale_shift(t, s)
                ins.then_inc(S["scaled"], 1)
                n_hi[0] += 1
                dve.wait_ge(S["scaled"], n_hi[0])
                dve.wait_ge(S["norm_hi"], n_hi[0])
                dve.tensor_tensor(dst_lo, stage16, dst_hi, ALU.subtract).then_inc(S["norm_ready"], 1)
                dve.wait_ge(S["norm_ready"], n_hi[0])

            def modulate(t, s):
                return dve.tensor_scalar(stage16[:, t, :], stage16[:, t, :], affine[:, 0, t, s:s + 1],
                                         affine[:, 1, t, s:s + 1], ALU.mult, ALU.add)

            def weigh(name):
                return lambda t, s: dve.tensor_scalar(stage16[:, t, :], stage16[:, t, :], col(name, t), A_SCALE,
                                                      ALU.mult, ALU.mult)

            for layer, L in enumerate(LAYERS):
                n, r0, s_n = L["n"], 4 * layer, L["n"] // TOK
                for half in range(2):
                    dve.wait_ge(bank_free[half], 1 + G0[L["conv"]] // 2)
                make_affine(layer)
                rstd_wait()
                for s, src in enumerate((x3, ctx3)):
                    norm_split(src, s, modulate, norm_op[0][:, :, s * TOK:(s + 1) * TOK],
                               norm_op[1][:, :, s * TOK:(s + 1) * TOK])

                dve.memset(pad[:, :, :, 0:1], 0.0)
                dve.memset(pad[:, :, :, 257:258], 0.0)
                link(dve.memset(conv_sum, 0.0))
                order = L["conv_order"]
                per, u0, g0 = len(order), U0[L["conv"]], G0[L["conv"]]
                h_t, z_t = pair(za, 0, 512), pair(za, 1024, 512)
                e_t, s_t = pair(zb, 0, 512), pair(zb, 1024, 512)
                mods = 0
                with dve.Fori(0, 4) as i:
                    chain.enter(i, 3 + 1 + 3)
                    for k, what in enumerate(order):
                        split_lo(i, per, u0 + k + 1)
                        group_wait(i, per, u0 + k) if what != "h" else None
                        bank = banks(k % 2, n)
                        if what == "M":
                            mod_out(i, 8, 48 + 2 * mods, k % 2)
                            mods += 1
                        if what == "c":
                            dve.wait_ge(S["conv_h"], i + (r0 + 1))
                            for m in range(2):
                                ins = stt(pad[:, m, 0:s_n, 1:257], bank[:, m, :].rearrange("p (s n) -> p s n", n=TOK),
                                          UNSCALE, h_t[:, m, 0:n].rearrange("p (s n) -> p s n", n=TOK),
                                          ALU.mult, ALU.mult)
                            ins.then_inc(S["conv_in"], 1)
                            dve.wait_ge(S["conv_in"], i + (r0 + 1) + 1)
                            dve.sem_inc(bank_free[k % 2], 1)
                            for tap in range(3):
                                for m in range(2):
                                    w = cols("conv_w", i, 2, (3 * layer + tap) * 8 + m)
                                    src = pad[:, m, 0:s_n, tap:tap + TOK]
                                    dst = conv_t[:, m * 512:m * 512 + n].rearrange("p (s n) -> p s n", n=TOK)
                                    if tap == 0:
                                        ins = dve.tensor_scalar(dst, src, w, None, ALU.mult)
                                    else:
                                        ins = stt(dst, src, w, dst, ALU.mult, ALU.add)
                                link(ins)
                        if what == "b":
                            stt(stage8[:, bass.ds(i * 2, 2), 0:n], bank, UNSCALE, pair(conv_t, 0, 512)[:, :, 0:n],
                                ALU.mult, ALU.mult).then_inc(S["conv_y"], 1)
                            dve.wait_ge(S["conv_y"], i + (r0 + 1))
                            dve.sem_inc(bank_free[k % 2], 1)
                        if what == "z":
                            dve.wait_ge(S["conv_sq"], i + (r0 + 1))
                            sq = pair(conv_sq, 0, 512)
                            link(dve.tensor_tensor(conv_sum[:, 0:n], conv_sum[:, 0:n], sq[:, 0, 0:n], ALU.add))
                            dve.tensor_tensor(conv_sum[:, 0:n], conv_sum[:, 0:n], sq[:, 1, 0:n], ALU.add)\
                               .then_inc(S["conv_sum"], 1)
                            dve.wait_ge(S["conv_sum"], i + (r0 + 1) + 1)
                            dve.wait_ge(S["conv_z"], i + (r0 + 1))
                            link(silu(z_t[:, :, 0:n], e_t[:, :, 0:n], s_t[:, :, 0:n]))
                            for m in range(2):
                                y = stage8[:, bass.ds(i * 2 + m, 1), 0:n]
                                ins = stt(y, y, cols("conv_norm_w", i, 2, 8 * layer + m), z_t[:, m:m + 1, 0:n],
                                          ALU.mult, ALU.mult)
                            ins.then_inc(S["conv_g"], 1)
                chain.leave(4)
                dve.wait_ge(S["conv_g"], r0 + 4 + 1)
                rstd_wait()
                dve.tensor_tensor(stage8[:, :, 0:n], stage8[:, :, 0:n], over(rstd[:, 0:n], 8), ALU.mult)\
                   .then_inc(S["conv_scaled"], 1)
                dve.wait_ge(S["conv_scaled"], layer + 1)
                dve.wait_ge(S["conv_hi"], layer + 1)
                stt(mix_op[1][:, 0:8, 0:n], stage8[:, :, 0:n], A_SCALE, mix_op[0][:, 0:8, 0:n],
                    ALU.mult, ALU.subtract).then_inc(S["conv_done"], 1)

                order = L["ret_order"]
                per, u0, g0 = len(order), U0[L["ret"]], G0[L["ret"]]
                mods = 0
                with dve.Fori(0, 4) as i:
                    chain.enter(i, 2 * 2 + 2 + 2 * 4)

                    def rope(buf, bank, which):
                        dve.wait_ge(S["rot_done"], i * 2 + (2 * r0 + which))
                        v = pair(buf, 0, 512)[:, :, 0:TOK]
                        t = pair(o_b, 0, TOK)
                        dve.tensor_tensor(t, aux[:, bank, :].rearrange("p (m n) -> p m n", m=2), over(sin, 2), ALU.mult)
                        link(dve.tensor_tensor(v, v, over(cos, 2), ALU.mult))
                        link(dve.tensor_tensor(v, v, t, ALU.add))
                        dve.sem_inc(S["roped"], 1)

                    for k, what in enumerate(order):
                        split_lo(i, per, u0 + k + 1)
                        if what == "M":
                            group_wait(i, per, u0 + k)
                            mod_out(i, 4, (32 if mods < 2 else 80) + 2 * (mods % 2), k % 2)
                            mods += 1
                        if what == "v":
                            rope(k_b, 0, 1)
                        if what == "z":
                            rope(q_b, 1, 2)
                    dve.wait_ge(S["z_sigmoid"], i + (r0 + 1))
                    z_t, e_t, s_t = (pair(b, 0, 512)[:, :, 0:n] for b in (z_b, e_b, s_b))
                    silu(z_t, e_t, s_t).then_inc(S["z_silu"], 1)
                    dve.wait_ge(S["z_silu"], i + (r0 + 1))
                    for h in range(2):
                        hd = i * 2 + (2 * r0 + h + 1)
                        dve.wait_ge(S["mask_exp"], i * 8 + (8 * r0 + 4 * h + 4))
                        dve.tensor_tensor(mask_x, mask_x, is_ge, ALU.mult)
                        dve.tensor_tensor(mask_c, mask_c, t2, ALU.add)
                        link(dve.tensor_tensor(t1, t1, is_le, ALU.mult))
                        link(dve.tensor_tensor(mask_x, mask_x, t1, ALU.add))
                        dve.wait_ge(S["scores_done"], hd)
                        dve.tensor_tensor(p_b[:, 0, :], aux[:, 0, :], mask_x, ALU.mult)
                        if n == 512:
                            dve.tensor_tensor(p_b[:, 2, :], aux[:, 2, :], mask_x, ALU.mult)
                        dve.tensor_tensor(p_b[:, 1, :], aux[:, 1, :], mask_c, ALU.mult).then_inc(S["p_ready"], 1)
                        dve.wait_ge(S["mean_psum"], hd)
                        stt(o_b[:, 0:n], aux[:, 0, 0:n], -1.0 / P, o_b[:, 0:n], ALU.mult, ALU.add)\
                            .then_inc(S["centered"], 1)
                        dve.wait_ge(S["centered"], hd)
                        dve.wait_ge(S["orstd_ready"], hd)
                        dve.wait_ge(S["osq_ready"], hd)
                        link(stt(o_b[:, 0:n], o_b[:, 0:n], cols("ret_norm_w", i, 2, 8 * layer + h), rstd[:, 0:n],
                                 ALU.mult, ALU.mult))
                        dve.tensor_tensor(o_b[:, 0:n], o_b[:, 0:n], z_b[:, h * 512:h * 512 + n], ALU.mult)\
                           .then_inc(S["y_ready"], 1)
                        dve.wait_ge(S["y_ready"], hd)
                        dve.wait_ge(S["y_hi"], hd)
                        tile = bass.ds(i * 2 + (8 + h), 1)
                        link(stt(mix_op[1][:, tile, 0:n], o_b[:, 0:n].rearrange("p (a n) -> p a n", a=1), A_SCALE,
                                 mix_op[0][:, tile, 0:n], ALU.mult, ALU.subtract))
                        dve.sem_inc(S["ret_done"], 1)
                chain.leave(4)

                if layer == 0:
                    make_gates()
                u0, g0 = U0[L["out"]], G0[L["out"]]
                with dve.Fori(0, 4) as i:
                    for k in range(2):
                        split_lo(i, 2, u0 + k + 1)
                        group_wait(i, 2, u0 + k)
                        for s in range(s_n):
                            for m in range(2):
                                res = (x3, ctx3)[s][:, bass.ds(i * 4 + (2 * k + m), 1), :]
                                gate = gates[:, bass.ds(i * 8 + (32 * layer + 2 * (2 * k + m) + s), 1)]
                                ins = stt(res, proj[:, 2 * k + m:2 * k + m + 1, s * TOK:(s + 1) * TOK], gate, res,
                                          ALU.mult, ALU.add)
                        ins.then_inc(bank_free[k], 1)
                dve.wait_ge(bank_free[1], (g0 + 7) // 2 + 2)
                dve.sem_inc(S["res_done"], 1)

            rstd_wait()
            link(dve.tensor_tensor(x3, x3, over(rstd[:, 0:TOK], KT), ALU.mult))
            for t in range(KT):
                ins = dve.tensor_scalar(x3[:, t, :], x3[:, t, :], col("final_norm_w", t), None, ALU.mult)
            link(ins)
            dve.sem_inc(S["res_done"], 1)
            rstd_wait()
            norm_split(x3, 0, weigh("mix_pre"), u_op[0], u_op[1])

            dve.wait_ge(S["dtw_hi"], 1)
            stt(dtw_lo, tmp[:, 0:512], W_SCALE, dtw_hi, ALU.mult, ALU.subtract).then_inc(S["dtw_lo"], 1)
            dve.wait_ge(S["dt_log"], 1)
            link(dve.tensor_scalar(dt_um, dt_e, 1.0, None, ALU.add))
            link(dve.tensor_scalar(dt_um, dt_um, -1.0, None, ALU.add))
            link(dve.tensor_scalar(dt_eq, dt_um, 0.0, None, ALU.is_equal))
            link(dve.tensor_tensor(dt_um, dt_um, dt_eq, ALU.add))
            link(dve.reciprocal(dt_um, dt_um))
            link(dve.tensor_tensor(dt_um, dt_um, dt_e, ALU.mult))
            link(dve.tensor_tensor(dt_l, dt_l, dt_um, ALU.mult))
            link(dve.tensor_tensor(dt_eq, dt_eq, dt_e, ALU.mult))
            link(dve.tensor_tensor(dt_l, dt_l, dt_eq, ALU.add))
            link(stt(dt_x, dt_x, 0.0, dt_l, ALU.max, ALU.add))
            dve.tensor_scalar(dt_a, dt_x, hcol[:, 2:3], -1.0, ALU.mult, ALU.mult).then_inc(S["dt_ready"], 1)
            dve.wait_ge(att_in, 16)
            dve.wait_ge(S["cum_ready"], 3)

            u0, g0 = U0["att"], G0["att"]
            with dve.Fori(0, 4) as i:
                chain.enter(i, 4 * 2)
                for k in range(6):
                    split_lo(i, 6, u0 + k + 1)
                    if k % 3 < 2:
                        continue
                    for m in range(2):
                        hd = i * 4 + (2 * (k // 3) + m + 1)
                        dve.wait_ge(S["att_scores"], hd)
                        link(dve.tensor_tensor(att_s, aux[:, 0, 0:384], att_log, ALU.add))
                        dve.tensor_reduce(att_m[:, 0:1], att_s[:, 0:128], AX.X, ALU.max, negate=True)
                        dve.tensor_reduce(att_m[:, 1:2], att_s[:, 128:384], AX.X, ALU.max, negate=True)\
                           .then_inc(S["att_max"], 1)
                        dve.wait_ge(S["att_exp"], i * 8 + (4 * (k // 3) + 2 * m + 2))
                        link(dve.reciprocal(att_r, att_sum))
                        dve.tensor_scalar(att_s[:, 0:128], att_s[:, 0:128], att_r[:, 0:1], None, ALU.mult)
                        dve.tensor_scalar(att_s[:, 128:384], att_s[:, 128:384], att_r[:, 1:2], None, ALU.mult)\
                           .then_inc(S["att_p"], 1)
                        dve.wait_ge(S["att_hi"], hd)
                        tile = bass.ds(i * 4 + (KT + 2 * (k // 3) + m), 1)
                        stt(mix2_op[1][:, tile, :], aux[:, 3:4, 0:TOK], A_SCALE, mix2_op[0][:, tile, :],
                            ALU.mult, ALU.subtract).then_inc(S["att_done"], 1)
            chain.leave(4)

            dve.wait_ge(S["att_done"], ATT_HEADS + 1)
            link(dve.memset(pad2[:, :, 0:3], 0.0))
            u0, g0 = U0["ssd"], G0["ssd"]
            with dve.Fori(0, 4) as i:
                chain.enter(i, 2 * (3 + 2 * (3 + 2) + 1))
                for k in range(6):
                    split_lo(i, 6, u0 + k + 1)
                    sub, what = k // 3, k % 3
                    if what == 0:
                        dve.wait_ge(S["zs_sigmoid"], i * 2 + (sub + 1))
                        link(silu(zs, zs_e, zs_s))
                        continue
                    q = what - 1
                    dve.wait_ge(S["xbc_pad"], i * 4 + (2 * sub + q + 1))
                    for tap in range(4):
                        for m in range(2):
                            per_i, tile = (4, 2 * sub + m) if q == 0 else (2, KT + 8 * m + sub)
                            dst, src = xbc[:, 2 * q + m, :], pad2[:, 2 * q + m, tap:tap + TOK]
                            w = cols("conv_w2", i, per_i, 32 * tap + tile)
                            if tap == 0:
                                ins = dve.tensor_scalar(dst, src, w, cols("conv_b2", i, per_i, tile),
                                                        ALU.mult, ALU.add)
                            else:
                                ins = stt(dst, src, w, dst, ALU.mult, ALU.add)
                        if tap < 3:
                            link(ins)
                    ins.then_inc(S["xbc_conv"], 1)
                    dve.wait_ge(S["xbc_conv"], i * 4 + (2 * sub + q + 1))
                    dve.wait_ge(S["xbc_sigmoid"], i * 4 + (2 * sub + q + 1))
                    silu(xbc[:, 2 * q:2 * q + 2, :], xbc_e[:, 2 * q:2 * q + 2, :], xbc_s[:, 2 * q:2 * q + 2, :])\
                        .then_inc(S["xbc_ready"], 1)
                    if q == 0:
                        continue

                    def row(r):
                        hd = i * 8 + (4 * sub + r)
                        dve.wait_ge(S["row_psum"], hd + 1)
                        dve.tensor_scalar(rows, acs, ident[0:SSM_HEADS, bass.ds(hd, 1)], None, ALU.mult)\
                           .then_inc(S["row_ready"], 1)

                    row(0)
                    dve.wait_ge(S["gram_psum"], i * 2 + (sub + 1))
                    for r in range(4):
                        if r < 3:
                            row(r + 1)
                        hd = i * 8 + (4 * sub + r)
                        dve.wait_ge(S["decay_ready"], i * 16 + 2 * (4 * sub + r + 1) + 1)
                        dve.wait_ge(S["pw_used"], hd + 1)
                        stt(pw[:, 0:TOK], aux[:, 1, 0:TOK], dt_t[:, bass.ds(hd, 1)], decay_w[:, 0:TOK],
                            ALU.mult, ALU.mult)
                        stt(pw[:, TOK:384], aux[:, 1, TOK:384], dt_t[:, bass.ds(i * 8 + (32 + 4 * sub + r), 1)],
                            decay_w[:, TOK:384], ALU.mult, ALU.mult).then_inc(S["pw_ready"], 1)
                    gr = i * 2 + (sub + 1)
                    dve.wait_ge(S["pw_used"], i * 8 + (4 * sub + 4) + 1)
                    for m in range(2):
                        ins = stt(yg[:, m, :], xbc[:, m, :], dsk[:, bass.ds(i * 4 + (2 * sub + m), 1)],
                                  aux[:, 3, m * TOK:(m + 1) * TOK], ALU.mult, ALU.add)
                    link(ins)
                    dve.tensor_tensor(yg, yg, zs, ALU.mult).then_inc(S["yg_ready"], 1)
                    dve.wait_ge(S["yg_ready"], gr)
                    dve.wait_ge(S["yg_rstd"], gr)
                    for m in range(2):
                        ins = stt(yg[:, m, :], yg[:, m, :], cols("ssm_norm_w", i, 4, 2 * sub + m), rstd[:, 0:TOK],
                                  ALU.mult, ALU.mult)
                    ins.then_inc(S["yg_norm"], 1)
                    dve.wait_ge(S["yg_norm"], gr)
                    dve.wait_ge(S["yg_hi"], gr)
                    tiles = bass.ds(i * 4 + 2 * sub, 2)
                    stt(mix2_op[1][:, tiles, :], yg, A_SCALE, mix2_op[0][:, tiles, :], ALU.mult, ALU.subtract)\
                        .then_inc(S["ssd_done"], 1)
            chain.leave(4)

            def add_normed(name, count):
                rstd_wait()
                dve.wait_ge(S["stage_ready"], count)
                link(dve.tensor_tensor(stage16, stage16, over(rstd[:, 0:TOK], KT), ALU.mult))
                for t in range(KT):
                    ins = stt(x3[:, t, :], stage16[:, t, :], col(name, t), x3[:, t, :], ALU.mult, ALU.add)
                link(ins)
                dve.sem_inc(S["res_done"], 1)

            with dve.Fori(0, 4) as i:
                for k in range(4):
                    split_lo(i, 4, U0["mixout"] + k + 1)
            add_normed("mix_post", 8)
            rstd_wait()
            norm_split(x3, 0, weigh("mlp_pre"), u_op[0], u_op[1])

            with dve.Fori(0, 16) as i:
                for k in range(2):
                    split_lo(i, 2, U0["up"] + k + 1)
                    group_wait(i, 2, U0["up"] + k)
                    dve.tensor_scalar(pair(tmp, 512 * k, TOK), banks(k, TOK), 0.0, UNSCALE, ALU.max, ALU.mult)\
                       .then_inc(S["relu_ready"], 1)
                    dve.wait_ge(S["relu_ready"], i * 2 + (k + 1))
                    dve.sem_inc(bank_free[k], 1)
                    dve.wait_ge(S["hid_hi"], i * 4 + (2 * k + 2))
                    tiles = bass.ds(i * 4 + 2 * k, 2)
                    dve.tensor_tensor(hid_op[1][:, tiles, :], pair(tmp, 1024 + 512 * k, TOK), hid_op[0][:, tiles, :],
                                      ALU.subtract).then_inc(S["hid_ready"], 1)

            with dve.Fori(0, 3) as i:
                for k in range(8):
                    split_lo(i, 8, U0["down"] + k + 1)
            for k in range(7):
                split_lo(3, 8, U0["down"] + k + 1)
            add_normed("mlp_post", 16)


def constants():
    part = np.arange(P)
    ident = np.eye(P, dtype=np.float32)
    quarter = P // 4
    rot = np.zeros((P, P), np.float32)
    first = (part // quarter) % 2 == 0
    rot[part[first] + quarter, part[first]] = -1.0
    rot[part[~first] - quarter, part[~first]] = 1.0
    inv = (np.float32(10000.0) ** (-np.arange(quarter, dtype=np.float32) / np.float32(quarter))).astype(np.float32)
    tok = np.arange(TOK)
    pos = np.where(part[:, None] < P // 2, tok // 64, tok % 64).astype(np.float32)
    ang = pos * inv[part % quarter][:, None]
    i, j = tok[:, None], tok[None, :]
    seen = sum(((j <= i) & (i - j <= w) & ((i - j) % d == 0)).astype(np.int64)
               for w, d in ((128, 1), (512, 4), (2048, 16)))
    log = np.where(seen > 0, np.log(np.maximum(seen, 1)), -1e30).astype(np.float32)
    f32 = np.concatenate([ident, np.ones((P, P), np.float32), rot, np.cos(ang), np.sin(ang),
                          log[0:P, 0:P], log[P:, :]], axis=1).astype(np.float32)
    diff = (tok[None, None, :] - (part[:, None] + P * np.arange(2)[None, :])[:, :, None]).reshape(P, 512)
    causal = np.where(part[None, :] >= part[:, None], 0.0, -1e30)
    bf = np.concatenate([diff, diff >= 0, np.maximum(diff, 0), np.maximum(-diff, 0), diff <= 0, ident, causal],
                        axis=1)
    return f32, bf.astype(mybir.dt.np(BF16))


def kernel(**inputs):
    import concourse.bacc as _bacc
    from concourse.bass_utils import run_bass_kernel_spmd as _run

    a = {k: np.asarray(v) for k, v in inputs.items()}

    def tiles(v):
        return np.ascontiguousarray(v.reshape(-1, P).T)

    def chunked(w, columns):
        w = w[:, columns] if columns is not None else w
        k, m = w.shape
        return w.reshape(k // (P * CHUNK_K), CHUNK_K, P, m // WCOL, WCOL).transpose(3, 0, 2, 1, 4)\
            .reshape(-1, P, CHUNK_K * WCOL)

    def interleave(order, parts, rounds):
        out = []
        for r in range(rounds):
            used = {name: 0 for name in parts}
            for name in order:
                n = len(parts[name]) // (rounds * order.count(name))
                at = r * n * order.count(name) + used[name] * n
                out.append(parts[name][at:at + n])
                used[name] += 1
        return out

    w_mod, w_in, w_in2 = a["w_mod"], a["w_in"], a["w_in_2"][0]
    mod = [chunked(w_mod[l], None) for l in range(2)]
    win = [[chunked(w_in[l][:, 1024 * b:1024 * (b + 1)], None) for b in range(8)] for l in range(2)]
    blocks = [mod[0][0:32]]
    for l in range(2):
        ah, ab, ac, az, q, k, v, rz = win[l]
        conv = dict(h=ah, c=ac, b=ab, z=az)
        ret = dict(k=k, q=q, v=v, z=rz)
        if l == 0:
            conv["M"] = mod[1][0:32]
            g0_, g1_ = mod[0][32:48].reshape(4, 4, P, -1), mod[1][32:48].reshape(4, 4, P, -1)
            ret["M"] = np.concatenate([g0_, g1_], axis=1).reshape(32, P, -1)
        blocks += interleave("hcMMbzMM" if l == 0 else "hcbz", conv, 4)
        blocks += interleave("kqMMvzMM" if l == 0 else "kqvz", ret, 4)
        blocks.append(chunked(a["w_out"][l], None))
    base = D + 2 * D
    q0 = base + SSM_HEADS
    qkv = {n: chunked(w_in2[:, q0 + D * j:q0 + D * (j + 1)], None) for j, n in enumerate("qkv")}
    blocks += interleave("qkv", qkv, 8)
    n_state = SSM_GROUPS * P
    bc = np.stack([w_in2[:, 2 * D:2 * D + n_state].reshape(D, SSM_GROUPS, P),
                   w_in2[:, 2 * D + n_state:2 * D + 2 * n_state].reshape(D, SSM_GROUPS, P)], axis=2)
    ssd = dict(z=chunked(w_in2[:, 0:D], None), x=chunked(w_in2[:, D:2 * D], None),
               B=chunked(bc.reshape(D, 2 * n_state), None))
    blocks += interleave("zxB", ssd, 8)
    blocks += [chunked(a[n][0], None) for n in ("w_out_2", "w_up_2", "w_down_2")]
    stream = np.concatenate(blocks, axis=0)
    assert stream.shape == (N_CHUNKS, P, CHUNK_K * WCOL), stream.shape

    order = ("norm_w", "b_mod", "conv_w", "conv_norm_w", "ret_norm_w", "final_norm_w", "norm_mix_pre_2",
             "ssm_norm_w_2", "norm_mix_post_2", "norm_mlp_pre_2", "norm_mlp_post_2", "conv_w_2", "conv_b_2",
             "c", "c_ctx")
    params = np.concatenate([tiles(a[n]) for n in order], axis=1)
    assert params.shape == (P, N_PCOLS)
    heads_row = np.concatenate([a["ret_decay_f"].reshape(-1), a["ret_decay_b"].reshape(-1)])
    ssm_cols = np.stack([a["dt_bias_2"][0], a["a_log_2"][0]], axis=1)
    dskip = np.repeat(a["d_skip_2"][0].reshape(KT, 2).T, 64, axis=0)
    dt_w = w_in2[:, base:q0].reshape(KT, P, SSM_HEADS).transpose(1, 0, 2).reshape(P, -1)

    def feature_major(v):
        return v[0].T.reshape(KT, P, TOK).transpose(1, 0, 2).reshape(P, KT * TOK)

    c_f32, c_bf = constants()
    arrays = dict(xT=feature_major(a["x"]), ctxT=feature_major(a["ctx"]), params=params, heads_row=heads_row,
                  ssm_cols=ssm_cols, dskip=dskip, stream=stream, dt_w=dt_w, c_f32=c_f32, c_bf=c_bf)
    arrays = {k: np.ascontiguousarray(v) for k, v in arrays.items()}
    nc = _bacc.Bacc("TRN2", target_bir_lowering=False, num_devices=1)
    args = {k: nc.dram_tensor(k, v.shape, mybir.dt.from_np(v.dtype), kind="ExternalInput").ap()
            for k, v in arrays.items()}
    out = nc.dram_tensor("out", (P, KT * TOK), F32, kind="ExternalOutput").ap()
    build(nc, out=out, **args)
    r = _run(nc, [arrays], core_ids=[0])
    y = r.results[0]["out"].reshape(P, KT, TOK).transpose(2, 1, 0).reshape(1, TOK, D)
    return np.ascontiguousarray(y)
```

```python
from contextlib import ExitStack

import concourse.bass as bass
import numpy as np
from concourse import mybir

P = 128
TOK = 256
D = 2048
KT = D // P
HEADS = 8
SSM_HEADS = 32
SSM_GROUPS = 8
ATT_HEADS = 16
EPS = 1e-6
CHUNK_K = 8
WCOL = 256
SLOTS = 4

W_SCALE = 256.0
A_SCALE = 16.0
UNSCALE = 1.0 / (W_SCALE * A_SCALE)
HEAD_SCALE = float(P) ** -0.5

F32 = mybir.dt.float32
F16 = mybir.dt.float16
BF16 = mybir.dt.bfloat16
ALU = mybir.AluOpType
ACT = mybir.ActivationFunctionType
AX = mybir.AxisListType

CHUNKS = dict(mod=32, conv0=96, ret0=32, out0=16, conv1=32, ret1=32, out1=16,
              att=48, ssd=48, mixout=32, up=64, down=64)
GROUPS = dict(mod=16, conv0=16, ret0=16, out0=8, conv1=16, ret1=16, out1=8,
              att=24, ssd=24, mixout=8, up=32, down=8)
C0, G0, _c, _g = {}, {}, 0, 0
for _name in CHUNKS:
    C0[_name], G0[_name] = _c, _g
    _c += CHUNKS[_name]
    _g += GROUPS[_name]
N_CHUNKS = _c
AHEAD = SLOTS - 1

PCOLS = {}
_c = 0
for _name, _n in (("norm_w", 2 * KT), ("b_mod", 2 * 48), ("conv_w", 2 * 3 * 8), ("conv_norm_w", 16),
                  ("ret_norm_w", 16), ("final_norm_w", KT), ("mix_pre", KT), ("ssm_norm_w", KT),
                  ("mix_post", KT), ("mlp_pre", KT), ("mlp_post", KT), ("conv_w2", 4 * 32),
                  ("conv_b2", 32), ("c", KT), ("c_ctx", KT)):
    PCOLS[_name] = _c
    _c += _n
N_PCOLS = _c


class Chain:

    def __init__(self, eng, sem):
        self.eng, self.sem, self.base, self.k, self.i, self.per = eng, sem, 0, 0, 0, 0

    def enter(self, i, per, start=0):
        self.base += self.k - start * per
        self.i, self.per, self.k = i, per, 0

    def leave(self, stop):
        assert self.k == self.per, (self.k, self.per)
        self.base += stop * self.per
        self.i, self.per, self.k = 0, 0, 0

    def link(self, ins):
        self.k += 1
        ins.then_inc(self.sem, 1)
        self.eng.wait_ge(self.sem, self.i * self.per + (self.base + self.k))


def build(nc, xT, ctxT, params, heads_row, ssm_cols, dskip, stream, dt_w, c_f32, c_bf, out):
    with ExitStack() as ctx:
        def sb(name, shape, dt=F32):
            return ctx.enter_context(nc.sbuf_tensor(name, shape, dt))

        def sem(name):
            return ctx.enter_context(nc.semaphore(name))

        raw = sb("raw", [P, SLOTS, CHUNK_K * WCOL])
        w_hi = sb("w_hi", [P, SLOTS, CHUNK_K * WCOL], F16)
        w_lo = sb("w_lo", [P, SLOTS, CHUNK_K * WCOL], F16)
        x_res = sb("x_res", [P, KT * TOK])
        ctx_res = sb("ctx_res", [P, KT * TOK])
        norm_hl = sb("norm_hl", [P, 2 * KT * 512], F16)
        mix_hl = sb("mix_hl", [P, 2 * KT * 512], F16)
        stage = sb("stage", [P, KT * TOK])
        tmp = sb("tmp", [P, 4096])
        par = sb("par", [P, N_PCOLS])
        lg_raw = sb("lg_raw", [P, 32])
        lg, lg256, lg_neg = sb("lg", [P, 32]), sb("lg256", [P, 32]), sb("lg_neg", [P, 32])
        hcol = sb("hcol", [SSM_HEADS, 4])
        modraw = sb("modraw", [P, 2 * 48 * 2])
        affine = sb("affine", [P, 2, KT, 2])
        gates = sb("gates", [P, 2 * KT * 2])
        cvec = sb("cvec", [P, KT, 2, 2], F16)
        rstd = sb("rstd", [P, 512])
        eps = sb("eps", [P, 1])
        cst = sb("cst", [P, 896])
        cbf = sb("cbf", [P, 2816], BF16)
        dsk = sb("dsk", [P, KT])

        ident, ones, rot = cst[:, 0:128], cst[:, 128:256], cst[:, 256:384]
        cos, sin = cst[:, 384:640], cst[:, 640:896]
        diff, is_ge, dpos, dneg, is_le = (cbf[:, 512 * n:512 * n + 512] for n in range(5))
        ident_bf, causal_bf = cbf[:, 2560:2688], cbf[:, 2688:2816]

        x3 = x_res[:, :].rearrange("p (t n) -> p t n", t=KT)
        ctx3 = ctx_res[:, :].rearrange("p (t n) -> p t n", t=KT)
        stage16 = stage[:, :].rearrange("p (t n) -> p t n", t=KT)
        stage8 = stage[:, :].rearrange("p (t n) -> p t n", t=8)
        norm_half = [norm_hl[:, h * 8192:(h + 1) * 8192] for h in range(2)]
        mix_half = [mix_hl[:, h * 8192:(h + 1) * 8192] for h in range(2)]
        norm_op = [a.rearrange("p (t n) -> p t n", t=KT) for a in norm_half]
        mix_op = [a.rearrange("p (t n) -> p t n", t=KT) for a in mix_half]
        mix2_op = [a.rearrange("p (t n) -> p t n", t=2 * KT) for a in mix_half]
        hid_op = [a[:, :].rearrange("p (t n) -> p t n", t=64) for a in (norm_hl, mix_hl)]
        u_half = ctx_res[:, :].bitcast(F16)
        u_op = [u_half[:, h * 4096:(h + 1) * 4096].rearrange("p (t n) -> p t n", t=KT) for h in range(2)]
        mix_f32 = mix_hl[:, :].bitcast(F32)
        sq512 = mix_f32.rearrange("p (t n) -> p t n", t=KT)
        sq256 = mix_f32[:, 0:4096].rearrange("p (t n) -> p t n", t=KT)

        proj = ctx.enter_context(nc.psum_tensor("proj", [P, 4, 512], F32))
        aux = ctx.enter_context(nc.psum_tensor("aux", [P, 4, 512], F32))

        params_in, x_in, ctx_in = sem("params_in"), sem("x_in"), sem("ctx_in")
        raw_in = [sem(f"raw_in{s}") for s in range(SLOTS)]
        hi_ready, lo_ready = sem("hi_ready"), sem("lo_ready")
        chunk_free = sem("chunk_free")
        bank_free = [sem("bank_free_even"), sem("bank_free_odd")]
        act_chain, dve_chain = sem("act_chain"), sem("dve_chain")
        out_done, att_in, dtw_in, heads_in = sem("out_done"), sem("att_in"), sem("dtw_in"), sem("heads_in")
        names = """c_sigmoid c_silu c_hi c_lo
            first_squares first_sum squares_ready sums_ready stat_done rstd_ready scaled norm_hi norm_ready
            mods_read conv_h conv_in conv_y conv_sq conv_sum conv_z conv_g conv_scaled conv_hi conv_done
            kvq_ready rot_done roped vt_psum vt_ready z_sigmoid z_silu mask_exp scores_done p_ready o_psum o_ready
            mean_psum centered osq_ready var_psum orstd_ready y_ready y_hi ret_done
            res_part tile_sq tile_sum x_block
            dtw_hi dtw_lo a_ready dt_psum dt_log dt_ready dt_psum_t dt_t cum_psum cum_ready tri_ready
            att_qkv att_vt_psum att_vt att_scores att_max att_exp att_p att_pt_psum att_pt att_o att_hi att_done
            zs_sigmoid zs_ready xbc_pad xbc_conv xbc_sigmoid xbc_ready xt_psum xt_ready gram_psum row_ready
            row_psum decay_ready pw_ready pw_used yg_ready yg_sq yg_psum yg_rstd yg_norm yg_hi ssd_done
            stage_ready relu_ready hid_hi hid_ready""".split()
        S = {n: sem(n) for n in names}
        FREE_AT_FIRST = ("first_sum", "conv_in", "conv_sum", "conv_g", "mods_read", "tile_sum")
        LAYERS = [dict(n=512, conv="conv0", ret="ret0", out="out0", window=6),
                  dict(n=256, conv="conv1", ret="ret1", out="out1", window=2)]
        WINDOWS = "kvzq"

        def wait_if(eng, semaphore, value):
            if not (isinstance(value, int) and value <= 0):
                eng.wait_ge(semaphore, value)

        def banks(half, n):
            return proj[:, 2 * half:2 * half + 2, 0:n]

        def pair(buf, at, n):
            return buf[:, at:at + 2 * n].rearrange("p (m n) -> p m n", m=2)

        def col(name, k=0):
            return par[:, PCOLS[name] + k:PCOLS[name] + k + 1]

        def cols(name, i, per, k):
            return par[:, bass.ds(i * per + (PCOLS[name] + k), 1)]

        za, zb = mix_hl[:, 4096:8192].bitcast(F32), mix_hl[:, 12288:16384].bitcast(F32)
        pad = tmp[:, 0:1032].rearrange("p (m s n) -> p m s n", m=2, s=2)
        conv_t = tmp[:, 1032:2056]
        conv_sum = tmp[:, 2056:2568]
        conv_sq = tmp[:, 2568:3592]

        k_b, q_b, vt_b, z_b = (stage[:, 1024 * n:1024 * n + 1024] for n in range(4))
        v_b, e_b, s_b = tmp[:, 0:1024], tmp[:, 1024:2048], tmp[:, 2048:3072]
        p_b = tmp[:, 0:1536].rearrange("p (a n) -> p a n", a=3)
        mask_x, mask_c = tmp[:, 1536:2048], tmp[:, 2048:2560]
        o_b = [tmp[:, 2560:3072], tmp[:, 0:512]]
        t_b = [tmp[:, 3072:3584], tmp[:, 3584:4096]]
        orstd = [rstd[:, :], tmp[:, 512:1024]]
        silu_c = tmp[:, 64:96]
        c_silu = silu_c.rearrange("p (s t) -> p t s", s=2)

        tile_squares, tile_total = pair(tmp, 0, 512), tmp[:, 1024:1536]
        first_squares = sq512[:, 0:2, :]
        block_sums = [tmp[:, 1536 + 256 * b:1792 + 256 * b] for b in range(4)]

        late = cbf[:, 512:2560].bitcast(F32)
        acs = late[0:SSM_HEADS, 0:384]
        dt_t = late[:, 384:448]
        neg_acs = late[:, 448:512]
        tri = late[:, 512:1024]
        att_log = cst[:, 256:640]
        dtw_hi, dtw_lo = (tmp[:, n:n + 256].bitcast(F16) for n in (512, 768))
        dt_x, dt_e, dt_l, dt_um, dt_eq, dt_a = (tmp[0:SSM_HEADS, n:n + 256] for n in range(1024, 2560, 256))
        adt_t = tmp[:, 2560:2624]

        free_f32 = norm_hl[:, :].bitcast(F32)
        att_qkv = [free_f32[:, n:n + 512] for n in (4096, 4608, 5120)]
        att_vt = free_f32[:, 5632:6144]
        att_s = [free_f32[:, 384 * m:384 * m + 384] for m in range(2)]
        att_pt = free_f32[:, 768:1152]
        att_m, att_sum, att_r = ([free_f32[:, n + 2 * m:n + 2 * m + 2] for m in range(2)] for n in (1152, 1156, 1160))

        zs = [pair(stage, 512 * b, TOK) for b in range(2)]
        zs_e, zs_s = pair(stage, 1024, TOK), pair(stage, 1536, TOK)
        pad2 = stage[:, 2048:3088].rearrange("p (m n) -> p m n", m=4)
        decay_w = [stage[:, 3088 + 384 * b:3472 + 384 * b] for b in range(2)]
        xbc = [tmp[:, 1024 * b:1024 * b + 1024].rearrange("p (m n) -> p m n", m=4) for b in range(2)]
        xbc_e, xbc_s = (tmp[:, n:n + 1024].rearrange("p (m n) -> p m n", m=4) for n in (2048, 3072))
        rows = free_f32[0:SSM_HEADS, 3504:3888]
        xt, yg, yg_sq = free_f32[:, 1200:1712], pair(free_f32, 1712, TOK), pair(free_f32, 2224, TOK)
        pw = [free_f32[:, 2736 + 384 * b:3120 + 384 * b] for b in range(2)]

        def ctx_stage(b):
            at = (b // 2) * 4096 + (b % 2) * 1024
            return mix_f32[:, at:at + 1024].rearrange("p (t n) -> p t n", t=4)

        NORM_ORDER = [[(s, b) for b in range(4) for s in range(2)], [(s, b) for s in range(2) for b in range(4)]]

        block = ctx.enter_context(nc.Block())

        @block.sync
        def _(sp):
            sp.dma_start(par[:, :], params).then_inc(params_in, 16)
            sp.dma_start(lg_raw[:, :], heads_row.partition_broadcast(P)).then_inc(heads_in, 16)
            for s in range(SLOTS):
                sp.dma_start(raw[:, s, :], stream[s, :, :]).then_inc(raw_in[s], 16)
            sp.dma_start(x_res[:, :], xT).then_inc(x_in, 16)
            sp.dma_start(ctx_res[:, :], ctxT).then_inc(ctx_in, 16)
            with sp.Fori(1, N_CHUNKS // SLOTS) as i:
                for s in range(SLOTS):
                    sp.wait_ge(lo_ready, i * SLOTS + (s + 1 - SLOTS))
                    sp.dma_start(raw[:, s, :], stream[bass.ds(i * SLOTS + s, 1), :, :].rearrange("a p n -> (a p) n"))\
                      .then_inc(raw_in[s], 16)
            for b in range(4):
                sp.wait_ge(S["x_block"], 8 + b + 1)
                sp.dma_start(out[:, 4 * TOK * b:4 * TOK * (b + 1)], x_res[:, 4 * TOK * b:4 * TOK * (b + 1)])\
                  .then_inc(out_done, 16)
            sp.wait_ge(out_done, 64)

        @block.scalar
        def _(act):
            chain = Chain(act, act_chain)
            link = chain.link

            def split_hi(i, per, c):
                slot = c % SLOTS
                act.wait_ge(raw_in[slot], i * (4 * per) + 16 * (c // SLOTS + 1))
                act.wait_ge(chunk_free, i * per + (c + 1))
                act.activation(w_hi[:, slot, :], raw[:, slot, :], ACT.Copy, scale=W_SCALE).then_inc(hi_ready, 1)

            def chunk_wait(i, per, c):
                act.wait_ge(chunk_free, i * per + (c + 1 + SLOTS))

            def evacuated(semaphore, count, half):
                act.wait_ge(semaphore, count)
                act.sem_inc(bank_free[half], 1)

            def bank_wait(i, per, g):
                act.wait_ge(bank_free[g % 2], i * (per // 2) + (g // 2 + 2))

            def sigmoid_parts(z, e, s):
                link(act.activation(e, z, ACT.Abs))
                link(act.activation(e, e, ACT.Exp, scale=-1.0))
                link(act.activation(s, e, ACT.Ln, bias=1.0))
                return act.activation(s, s, ACT.Exp, scale=-1.0)

            n_stat, n_scaled = [0], [0]

            def make_rstd(n, count):
                n_stat[0] += 1
                act.wait_ge(S["stat_done"], n_stat[0])
                link(act.activation(rstd[:, 0:n], aux[:, 0, 0:n], ACT.Ln, bias=eps[:, :], scale=1.0 / count))
                act.activation(rstd[:, 0:n], rstd[:, 0:n], ACT.Exp, scale=-0.5).then_inc(S["rstd_ready"], 1)

            def norm_hi(blocks):
                for dst, src in blocks:
                    n_scaled[0] += 1
                    act.wait_ge(S["scaled"], n_scaled[0])
                    act.activation(dst, src, ACT.Copy).then_inc(S["norm_hi"], 1)

            def tiles4(op, b, s=0):
                return op[:, 4 * b:4 * b + 4, s * TOK:(s + 1) * TOK]

            act.dma_start(cst[:, :], c_f32[:, 0:896]).then_inc(params_in, 16)
            act.dma_start(cbf[:, :], c_bf).then_inc(params_in, 16)
            act.dma_start(dsk[:, :], dskip).then_inc(params_in, 16)
            act.dma_start(hcol[:, 0:2], ssm_cols).then_inc(params_in, 16)
            act.preload_act_table_set("natural_log_exp_and_others")
            act.wait_ge(params_in, 80)
            sigmoid_parts(par[:, PCOLS["c"]:PCOLS["c"] + 32], tmp[:, 0:32], tmp[:, 32:64]).then_inc(S["c_sigmoid"], 1)
            for c in range(AHEAD):
                split_hi(0, 0, c)
            act.wait_ge(S["c_silu"], 1)
            act.activation(cvec[:, :, :, 0], c_silu, ACT.Copy, scale=A_SCALE).then_inc(S["c_hi"], 1)
            act.wait_ge(heads_in, 16)
            link(act.activation(lg[:, :], lg_raw[:, :], ACT.Exp))
            link(act.activation(lg[:, :], lg[:, :], ACT.Copy, scale=-1.0))
            link(act.activation(lg256[:, :], lg[:, :], ACT.Copy, scale=float(TOK)))
            link(act.activation(lg_neg[:, :], lg[:, :], ACT.Copy, scale=-1.0))

            with act.Fori(0, 8) as i:
                for c in range(4):
                    split_hi(i, 4, c + AHEAD)
                    if c == 1:
                        act.wait_ge(x_in, 16)
                        act.wait_ge(ctx_in, 16)
                        act.wait_ge(S["first_sum"], i + 1)
                        for s, part in enumerate((x3, ctx3)):
                            ins = act.activation(first_squares[:, :, s * TOK:(s + 1) * TOK],
                                                 part[:, bass.ds(i * 2, 2), :], ACT.Square)
                        ins.then_inc(S["first_squares"], 1)
            make_rstd(512, D)

            for layer, L in enumerate(LAYERS):
                n, r0, win = L["n"], 4 * layer, L["window"]
                if layer:
                    make_rstd(512, D)
                norm_hi([(tiles4(norm_op[0], b, s), ctx_stage(b) if s else tiles4(stage16, b))
                         for s, b in NORM_ORDER[layer]])

                per, c0, g0 = 4 * win, C0[L["conv"]], G0[L["conv"]]
                h_t, z_t = pair(za, 0, 512)[:, :, 0:n], pair(za, 1024, 512)[:, :, 0:n]
                e_t, s_t = pair(zb, 0, 512)[:, :, 0:n], pair(zb, 1024, 512)[:, :, 0:n]
                with act.Fori(0, 4) as i:
                    chain.enter(i, 3)
                    for c in range(per):
                        split_hi(i, per, c0 + c + AHEAD)
                        w = c // win
                        if c % win != win // 2:
                            continue
                        if w == 0:
                            chunk_wait(i, per, c0 + c)
                            act.wait_ge(S["conv_in"], i + (r0 + 1))
                            act.activation(h_t, banks(0, n), ACT.Copy, scale=UNSCALE).then_inc(S["conv_h"], 1)
                            evacuated(S["conv_h"], i + (r0 + 1), 0)
                        if w == 3:
                            act.wait_ge(S["conv_y"], i + (r0 + 1))
                            act.wait_ge(S["conv_sum"], i + (r0 + 1))
                            act.activation(pair(conv_sq, 0, 512)[:, :, 0:n], stage8[:, bass.ds(i * 2, 2), 0:n],
                                           ACT.Square).then_inc(S["conv_sq"], 1)
                            chunk_wait(i, per, c0 + c)
                            act.wait_ge(S["conv_g"], i + (r0 + 1))
                            act.activation(z_t, banks(1, n), ACT.Copy, scale=UNSCALE).then_inc(bank_free[1], 1)
                            bank_wait(i, 4, g0 + 3)
                            sigmoid_parts(z_t, e_t, s_t).then_inc(S["conv_z"], 1)
                chain.leave(4)
                make_rstd(n, D // 2)
                act.wait_ge(S["conv_scaled"], layer + 1)
                act.activation(mix_op[0][:, 0:8, 0:n], stage8[:, :, 0:n], ACT.Copy, scale=A_SCALE)\
                   .then_inc(S["conv_hi"], 1)

                def masks(i, d, h):
                    at = layer * 8 + 2 * d + h
                    fwd, bwd = bass.ds(i * 2 + at, 1), bass.ds(i * 2 + (16 + at), 1)
                    act.activation(mask_x, dpos, ACT.Exp, scale=lg[:, fwd]).then_inc(S["mask_exp"], 1)
                    act.activation(t_b[0], dneg, ACT.Exp, scale=lg[:, bwd]).then_inc(S["mask_exp"], 1)
                    act.activation(mask_c, diff, ACT.Exp, scale=lg[:, fwd], bias=lg256[:, fwd])\
                       .then_inc(S["mask_exp"], 1)
                    act.activation(t_b[1], diff, ACT.Exp, scale=lg_neg[:, bwd], bias=lg256[:, bwd])\
                       .then_inc(S["mask_exp"], 1)

                def ret_heads(step, i, d):
                    hd = [i * 2 + (2 * (r0 + d) + h + 1) for h in range(2)]
                    if step == 0:
                        act.wait_ge(S["vt_psum"], i + (r0 + d + 1))
                        act.activation(vt_b, aux[:, 2:4, :], ACT.Copy).then_inc(S["vt_ready"], 1)
                        act.wait_ge(S["z_silu"], i + (r0 + d + 1))
                        masks(i, d, 0)
                    if step == 1:
                        act.wait_ge(S["p_ready"], hd[0])
                        masks(i, d, 1)
                        for h in range(2):
                            act.wait_ge(S["o_psum"], hd[h])
                            act.activation(o_b[h][:, 0:n], aux[:, 3, 0:n], ACT.Copy).then_inc(S["o_ready"], 1)
                    if step == 2:
                        for h in range(2):
                            act.wait_ge(S["centered"], hd[h])
                            act.activation(t_b[h][:, 0:n], o_b[h][:, 0:n], ACT.Square).then_inc(S["osq_ready"], 1)
                    if step == 3:
                        for h in range(2):
                            act.wait_ge(S["var_psum"], hd[h])
                            link(act.activation(orstd[h][:, 0:n], aux[:, 2 + h, 0:n], ACT.Ln, bias=eps[:, :],
                                                scale=1.0 / P))
                            act.activation(orstd[h][:, 0:n], orstd[h][:, 0:n], ACT.Exp, scale=-0.5)\
                               .then_inc(S["orstd_ready"], 1)
                        for h in range(2):
                            act.wait_ge(S["y_ready"], hd[h])
                            act.activation(mix_op[0][:, bass.ds(i * 2 + (8 + 2 * d + h), 1), 0:n],
                                           o_b[h][:, 0:n].rearrange("p (a n) -> p a n", a=1), ACT.Copy,
                                           scale=A_SCALE).then_inc(S["y_hi"], 1)

                c0, g0 = C0[L["ret"]], G0[L["ret"]]

                def ret_round(i, heads):
                    for c in range(8):
                        split_hi(i, 8, c0 + c + AHEAD)
                        if heads and c < 4:
                            ret_heads(c, i, -1)
                        if c % 2 == 0:
                            continue
                        what, half = WINDOWS[c // 2], (c // 2) % 2
                        chunk_wait(i, 8, c0 + c)
                        if what == "z":
                            act.activation(pair(z_b, 0, 512)[:, :, 0:n], banks(half, n), ACT.Copy, scale=UNSCALE)\
                               .then_inc(bank_free[half], 1)
                            bank_wait(i, 4, g0 + 2)
                            sigmoid_parts(*(pair(b, 0, 512)[:, :, 0:n] for b in (z_b, e_b, s_b)))\
                                .then_inc(S["z_sigmoid"], 1)
                            continue
                        if what == "v" and heads:
                            act.wait_ge(S["ret_done"], i * 2 + 2 * r0)
                        m = n if what == "q" else 512
                        act.activation(pair({"k": k_b, "v": v_b, "q": q_b}[what], 0, 512)[:, :, 0:m], banks(half, m),
                                       ACT.Copy, scale=UNSCALE * (HEAD_SCALE if what == "k" else 1.0))\
                           .then_inc(S["kvq_ready"], 1)
                        evacuated(S["kvq_ready"], i * 3 + (3 * r0 + "kvq".index(what) + 1), half)

                act.wait_ge(S["conv_done"], layer + 1)
                ret_round(0, False)
                with act.Fori(1, 4) as i:
                    chain.enter(i, 5, 1)
                    ret_round(i, True)
                chain.leave(4)

                c0, t0 = C0[L["out"]], 8 * layer

                def out_round(i, heads):
                    for c in range(4):
                        split_hi(i, 4, c0 + c + AHEAD)
                        if heads and c < 3:
                            for step in ((0,), (1,), (2, 3))[c]:
                                ret_heads(step, 4, -1)
                        if c < 2:
                            continue
                        k = c - 2
                        act.wait_ge(S["res_part"], i * 2 + (t0 + k + 1))
                        act.wait_ge(S["tile_sum"], i * 2 + (t0 + k + 1))
                        for s in range(n // TOK):
                            ins = act.activation(tile_squares[:, :, s * TOK:(s + 1) * TOK],
                                                 (x3, ctx3)[s][:, bass.ds(i * 4 + 2 * k, 2), :], ACT.Square)
                        ins.then_inc(S["tile_sq"], 1)

                out_round(0, True)
                with act.Fori(1, 4) as i:
                    out_round(i, False)

            make_rstd(TOK, D)
            act.dma_start(tmp[:, 0:512], dt_w).then_inc(dtw_in, 16)
            act.dma_start(att_log, c_f32[:, 896:1280]).then_inc(att_in, 16)
            n_block = [0]

            def block_squares():
                for b in range(4):
                    n_block[0] += 1
                    act.wait_ge(S["x_block"], n_block[0])
                    act.activation(tiles4(sq256, b), tiles4(x3, b), ACT.Square).then_inc(S["squares_ready"], 1)

            block_squares()
            make_rstd(TOK, D)
            norm_hi([(tiles4(u_op[0], b), tiles4(stage16, b)) for b in range(4)])

            def step_sizes(step):
                if step == 0:
                    act.wait_ge(dtw_in, 16)
                    act.activation(dtw_hi, tmp[:, 0:512], ACT.Copy, scale=W_SCALE).then_inc(S["dtw_hi"], 1)
                    act.activation(tri, is_ge, ACT.Copy).then_inc(S["tri_ready"], 1)
                    act.activation(hcol[:, 2:3], hcol[:, 1:2], ACT.Exp).then_inc(S["a_ready"], 1)
                if step == 2:
                    act.wait_ge(S["dt_psum"], 1)
                    link(act.activation(dt_x, aux[0:32, 1, 0:TOK], ACT.Identity, scale=UNSCALE, bias=hcol[:, 0:1]))
                    link(act.activation(dt_e, dt_x, ACT.Abs))
                    link(act.activation(dt_e, dt_e, ACT.Exp, scale=-1.0))
                    act.activation(dt_l, dt_e, ACT.Ln, bias=1.0).then_inc(S["dt_log"], 1)
                if step == 4:
                    act.wait_ge(S["dt_psum_t"], 1)
                    act.activation(dt_t, aux[:, 2, 0:64], ACT.Copy).then_inc(S["dt_t"], 1)
                    act.activation(adt_t, aux[:, 2, 64:128], ACT.Copy).then_inc(S["dt_t"], 1)
                if step == 5:
                    act.wait_ge(S["cum_psum"], 1)
                    act.activation(acs[:, 0:256], aux[0:32, 3, 0:256], ACT.Copy).then_inc(S["cum_ready"], 1)
                    act.activation(acs[:, 256:384], aux[0:32, 3, 128:256], ACT.Copy).then_inc(S["cum_ready"], 1)
                    act.activation(neg_acs, aux[:, 3, 256:320], ACT.Copy, scale=-1.0).then_inc(S["cum_ready"], 1)

            def att_heads(step, i, g):
                hd = [i * 4 + (2 * g + m + 1) for m in range(2)]

                def exps(m):
                    act.wait_ge(S["att_max"], hd[m])
                    for part, (a, b) in enumerate(((0, 128), (128, 384))):
                        act.activation(att_s[m][:, a:b], att_s[m][:, a:b], ACT.Exp, bias=att_m[m][:, part:part + 1],
                                       accum_out=att_sum[m][:, part:part + 1]).then_inc(S["att_exp"], 1)

                def take_pt(m):
                    act.wait_ge(S["att_pt_psum"], hd[m])
                    act.activation(att_pt, aux[:, 1, 0:384], ACT.Copy).then_inc(S["att_pt"], 1)

                def take_o(m):
                    act.wait_ge(S["att_o"], hd[m])
                    act.activation(mix2_op[0][:, bass.ds(i * 4 + (KT + 2 * g + m), 1), :], aux[:, 3:4, 0:TOK],
                                   ACT.Copy, scale=A_SCALE).then_inc(S["att_hi"], 1)

                if step == 0:
                    act.wait_ge(S["att_vt_psum"], i * 2 + (g + 1))
                    act.activation(att_vt, aux[:, 2, :], ACT.Copy).then_inc(S["att_vt"], 1)
                    exps(0)
                if step == 1:
                    take_pt(0)
                    exps(1)
                if step == 2:
                    take_o(0)
                    take_pt(1)
                if step == 3:
                    take_o(1)

            c0, g0 = C0["att"], G0["att"]

            def att_round(i, heads):
                for c in range(12):
                    split_hi(i, 12, c0 + c + AHEAD)
                    sub, step = c // 6, c % 6
                    if (heads or sub) and step < 4:
                        att_heads(step, i, sub - 1)
                    if not heads and not sub:
                        step_sizes(step)
                    if step % 2 == 0:
                        continue
                    what, half = step // 2, (c // 2) % 2
                    chunk_wait(i, 12, c0 + c)
                    act.activation(pair(att_qkv[what], 0, TOK), banks(half, TOK), ACT.Copy,
                                   scale=UNSCALE * (HEAD_SCALE if what == 0 else 1.0)).then_inc(S["att_qkv"], 1)
                    evacuated(S["att_qkv"], i * 6 + (3 * sub + what + 1), half)

            att_round(0, False)
            with act.Fori(1, 4) as i:
                att_round(i, True)

            def ssd_heads(step, i, g):
                gr, b = i * 2 + g, g % 2

                def decays(r):
                    hd = i * 8 + (4 * g + r)
                    act.wait_ge(S["row_psum"], hd + 1)
                    wait_if(act, S["pw_ready"], hd - 1)
                    act.activation(decay_w[r % 2][:, 0:256], aux[:, 2, 0:256], ACT.Exp,
                                   bias=neg_acs[:, bass.ds(hd, 1)]).then_inc(S["decay_ready"], 1)
                    act.activation(decay_w[r % 2][:, 256:384], aux[:, 2, 256:384], ACT.Exp,
                                   bias=neg_acs[:, bass.ds(hd + 32, 1)]).then_inc(S["decay_ready"], 1)

                if step == "sigmoid":
                    act.wait_ge(S["xbc_conv"], gr * 2 + 2)
                    wait_if(act, S["xbc_ready"], gr)
                    sigmoid_parts(xbc[b], xbc_e, xbc_s).then_inc(S["xbc_sigmoid"], 1)
                if step == 2:
                    decays(0)
                    act.wait_ge(S["xt_psum"], gr + 1)
                    act.activation(xt, aux[:, 0, :], ACT.Copy).then_inc(S["xt_ready"], 1)
                    decays(1)
                if step == 3:
                    decays(2)
                    decays(3)
                if step == 4:
                    act.wait_ge(S["yg_ready"], gr + 1)
                    act.activation(yg_sq, yg, ACT.Square).then_inc(S["yg_sq"], 1)
                if step == 5:
                    act.wait_ge(S["yg_psum"], gr + 1)
                    link(act.activation(rstd[:, 0:TOK], aux[:, 0, 0:TOK], ACT.Ln, bias=eps[:, :], scale=1.0 / 256))
                    act.activation(rstd[:, 0:TOK], rstd[:, 0:TOK], ACT.Exp, scale=-0.5).then_inc(S["yg_rstd"], 1)
                if step == "take":
                    act.wait_ge(S["yg_norm"], gr + 1)
                    act.activation(mix2_op[0][:, bass.ds(i * 4 + 2 * g, 2), :], yg, ACT.Copy, scale=A_SCALE)\
                       .then_inc(S["yg_hi"], 1)

            c0, g0 = C0["ssd"], G0["ssd"]

            def ssd_round(i, heads):
                for c in range(12):
                    sub, step, half = c // 6, c % 6, (c // 2) % 2
                    gr, busy = i * 2 + sub, heads or sub
                    if busy and step in (2, 3, 4, 5):
                        ssd_heads(step, i, sub - 1)
                    split_hi(i, 12, c0 + c + AHEAD)
                    if busy and step == 0:
                        ssd_heads("sigmoid", i, sub - 1)
                    if not busy and step < 4:
                        att_heads(step, 4, -1)
                    if step == 1:
                        chunk_wait(i, 12, c0 + c)
                        wait_if(act, S["ssd_done"], gr - 1)
                        act.activation(zs[sub], banks(half, TOK), ACT.Copy, scale=UNSCALE)\
                           .then_inc(bank_free[half], 1)
                    if step == 3:
                        wait_if(act, S["zs_ready"], gr)
                        bank_wait(i, 6, g0 + c // 2 - 1)
                        sigmoid_parts(zs[sub], zs_e, zs_s).then_inc(S["zs_sigmoid"], 1)
                    if step in (3, 5):
                        q = step // 2 - 1
                        chunk_wait(i, 12, c0 + c)
                        wait_if(act, S["xbc_conv"], gr * 2 + (q - 1))
                        act.activation(pad2[:, 2 * q:2 * q + 2, 3:3 + TOK], banks(half, TOK), ACT.Copy, scale=UNSCALE)\
                           .then_inc(S["xbc_pad"], 1)
                        evacuated(S["xbc_pad"], gr * 2 + (q + 1), half)
                    if busy and step == 5:
                        ssd_heads("take", i, sub - 1)

            ssd_round(0, False)
            with act.Fori(1, 4) as i:
                chain.enter(i, 2 * (3 + 3 + 1), 1)
                ssd_round(i, True)
            chain.leave(4)

            def take_stage(i, g, first):
                act.wait_ge(S["tile_sum"], i * 2 + (16 + first + g + 1))
                act.activation(stage16[:, bass.ds(i * 4 + 2 * g, 2), :], banks(g, TOK), ACT.Copy, scale=UNSCALE)\
                   .then_inc(S["stage_ready"], 1)
                evacuated(S["stage_ready"], i * 2 + (first + g + 1), g)
                act.activation(tile_squares[:, :, 0:TOK], stage16[:, bass.ds(i * 4 + 2 * g, 2), :], ACT.Square)\
                   .then_inc(S["tile_sq"], 1)

            c0 = C0["mixout"]

            def mix_round(i, heads):
                for c in range(8):
                    split_hi(i, 8, c0 + c + AHEAD)
                    if heads and c < 4:
                        for step in (("sigmoid",), (), (2,), (3, 4, 5, "take"))[c]:
                            ssd_heads(step, 4, -1)
                    if c in (5, 7):
                        chunk_wait(i, 8, c0 + c)
                        take_stage(i, (c - 5) // 2, 0)

            mix_round(0, True)
            with act.Fori(1, 4) as i:
                mix_round(i, False)
            make_rstd(TOK, D)
            block_squares()
            make_rstd(TOK, D)
            norm_hi([(tiles4(u_op[0], b), tiles4(stage16, b)) for b in range(4)])

            with act.Fori(0, 16) as i:
                for c in range(4):
                    split_hi(i, 4, C0["up"] + c + AHEAD)
                    if c % 2 == 0:
                        continue
                    k = c // 2
                    act.wait_ge(S["relu_ready"], i * 2 + (k + 1))
                    hid_t = pair(tmp, 1024 + 512 * k, TOK)
                    act.activation(hid_t, pair(tmp, 512 * k, TOK), ACT.Square, scale=A_SCALE ** 0.5)\
                       .then_inc(S["hid_hi"], 1)
                    act.wait_ge(S["hid_hi"], i * 4 + (2 * k + 1))
                    act.activation(hid_op[0][:, bass.ds(i * 4 + 2 * k, 2), :], hid_t, ACT.Copy)\
                       .then_inc(S["hid_hi"], 1)

            def down_round(i, last):
                for c in range(16):
                    if not (last and c + AHEAD >= 16):
                        split_hi(i, 16, C0["down"] + c + AHEAD)
                    if c % 8 == 7:
                        chunk_wait(i, 16, C0["down"] + c)
                        take_stage(i, c // 8, 8)

            with act.Fori(0, 3) as i:
                down_round(i, False)
            down_round(3, True)
            make_rstd(TOK, D)


        @block.tensor
        def _(pe):
            def chunk(i, per, c, n, op, kt0, half, first, last, hooks={}, ready=None):
                slot = c % SLOTS
                pe.wait_ge(lo_ready, i * per + (c + 1))
                for t in range(CHUNK_K):
                    if t in hooks:
                        hooks[t]()
                    if ready and t % 4 == 0:
                        ready(kt0 + t)
                    for m in range(2):
                        acc = proj[:, 2 * half + m, 0:n]
                        hi = w_hi[:, slot, t * WCOL + m * P:t * WCOL + (m + 1) * P]
                        lo = w_lo[:, slot, t * WCOL + m * P:t * WCOL + (m + 1) * P]
                        begin, end = first and t == 0, last and t == CHUNK_K - 1
                        pe.matmul(acc, hi, op[0][:, kt0 + t, 0:n], start=begin, stop=False)
                        pe.matmul(acc, hi, op[1][:, kt0 + t, 0:n], start=False, stop=False)
                        mm = pe.matmul(acc, lo, op[0][:, kt0 + t, 0:n], start=False, stop=end)
                mm.then_inc(chunk_free, 1)

            def mod_chunk(i, per, c, part, acc):
                slot = c % SLOTS
                pe.wait_ge(lo_ready, i * per + (c + 1))
                for t in range(CHUNK_K):
                    kt = CHUNK_K * part + t
                    vec = cvec[:, kt, :, :].rearrange("p s h -> p (s h)")
                    for m in range(2):
                        for w in (w_hi, w_lo):
                            mm = pe.matmul(acc[m], w[:, slot, t * WCOL + m * P:t * WCOL + (m + 1) * P], vec,
                                           start=kt == 0 and w is w_hi, stop=kt == KT - 1 and w is w_lo)
                mm.then_inc(chunk_free, 1)

            def bank_wait(i, per, g):
                pe.wait_ge(bank_free[g % 2], i * (per // 2) + (g // 2 + 1))

            n_stat, n_sums, n_norm = [0], [0], [0]

            def tile_stat(n, total=tile_total):
                n_stat[0] += 1
                pe.matmul(aux[:, 0, 0:n], ones, total[:, 0:n], start=True, stop=True).then_inc(S["stat_done"], 1)

            def block_stat():
                n_stat[0] += 1
                for b in range(4):
                    n_sums[0] += 1
                    pe.wait_ge(S["sums_ready"], n_sums[0])
                    mm = pe.matmul(aux[:, 0, 0:TOK], ones, block_sums[b], start=b == 0, stop=b == 3)
                mm.then_inc(S["stat_done"], 1)

            def normed(blocks, step):
                return lambda kt: pe.wait_ge(S["norm_ready"], blocks + step * (kt // 4 + 1))

            pe.sem_inc(chunk_free, SLOTS)
            pe.sem_inc(bank_free[0], 1)
            pe.sem_inc(bank_free[1], 1)
            pe.wait_ge(params_in, 80)
            pe.wait_ge(S["c_lo"], 1)
            with pe.Fori(0, 8) as i:
                for k in range(2):
                    bank_wait(i, 2, k)
                    for part in range(2):
                        mod_chunk(i, 4, 2 * k + part, part, [proj[:, 2 * k + m, 0:4] for m in range(2)])
            pe.wait_ge(S["first_sum"], 8 + 1)
            tile_stat(512)
            pe.wait_ge(S["rstd_ready"], n_stat[0])

            for layer, L in enumerate(LAYERS):
                n, r0, win = L["n"], 4 * layer, L["window"]
                if layer:
                    pe.wait_ge(S["tile_sum"], 8 + 1)
                    tile_stat(512)

                per, c0, g0 = 4 * win, C0[L["conv"]], G0[L["conv"]]
                with pe.Fori(0, 4) as i:
                    for w in range(4):
                        bank_wait(i, 4, g0 + w)
                        for part in range(2):
                            c = c0 + w * win + part * (win // 2)
                            ready = normed(8 * layer, 2 - layer) if w == 0 else None
                            chunk(i, per, c, n, norm_op, 8 * part, w % 2, part == 0, part == 1, ready=ready)
                            if layer:
                                continue
                            if part == 0:
                                pe.wait_ge(S["mods_read"], i * 8 + (2 * w + 1))
                            for u in range(2):
                                mod_chunk(i, per, c + 1 + u, part, [aux[:, 2 * u + m, 0:4] for m in range(2)])

                def conv_stat():
                    if layer == 0:
                        pe.wait_ge(S["mods_read"], 32 + 1)
                    pe.wait_ge(S["conv_sum"], r0 + 4 + 1)
                    tile_stat(n, conv_sum)

                def rotate(src, bank):
                    pe.matmul(aux[:, bank, :], rot, pair(src, 0, 512)[:, :, 0:TOK], start=True, stop=True)\
                      .then_inc(S["rot_done"], 1)

                def scores(h):
                    kk, qq = k_b[:, h * 512:(h + 1) * 512], q_b[:, h * 512:(h + 1) * 512]
                    for j in range(2):
                        pe.matmul(aux[:, 0, j * TOK:(j + 1) * TOK], kk[:, j * P:(j + 1) * P], qq[:, 0:TOK],
                                  start=True, stop=True)
                    for j in range(2):
                        ck = kk[:, TOK + j * P:TOK + (j + 1) * P]
                        mm = pe.matmul(aux[:, 1, j * TOK:(j + 1) * TOK], ck, qq[:, 0:TOK], start=True, stop=True)
                        if n == 512:
                            mm = pe.matmul(aux[:, 2, j * TOK:(j + 1) * TOK], ck, qq[:, TOK:512],
                                           start=True, stop=True)
                    mm.then_inc(S["scores_done"], 1)

                def values(h):
                    vt = [vt_b[:, h * 512 + j * P:h * 512 + (j + 1) * P] for j in range(4)]
                    for j in range(4):
                        mm = pe.matmul(aux[:, 3, 0:TOK], vt[j], p_b[:, j // 2, (j % 2) * TOK:(j % 2 + 1) * TOK],
                                       start=j == 0, stop=j == 3)
                    if n == 512:
                        for j in range(2):
                            mm = pe.matmul(aux[:, 3, TOK:512], vt[2 + j], p_b[:, 2, j * TOK:(j + 1) * TOK],
                                           start=j == 0, stop=j == 1)
                    mm.then_inc(S["o_psum"], 1)

                def ret_heads(step, i, d):
                    hd = [i * 2 + (2 * (r0 + d) + h + 1) for h in range(2)]
                    if step == "transpose":
                        pe.wait_ge(S["kvq_ready"], i * 3 + (3 * (r0 + d) + 3))
                        rotate(q_b, 1)
                        for h in range(2):
                            for j in range(4):
                                mm = pe.transpose(aux[:, 2 + h, j * P:(j + 1) * P],
                                                  v_b[:, h * 512 + j * P:h * 512 + (j + 1) * P], ident)
                        mm.then_inc(S["vt_psum"], 1)
                    if step == "scores0":
                        pe.wait_ge(S["roped"], i * 2 + (2 * (r0 + d) + 2))
                        pe.wait_ge(S["vt_ready"], i + (r0 + d + 1))
                        scores(0)
                    if step == "values0":
                        pe.wait_ge(S["p_ready"], hd[0])
                        values(0)
                        scores(1)
                    if step == "values1":
                        pe.wait_ge(S["p_ready"], hd[1])
                        pe.wait_ge(S["o_ready"], hd[0])
                        values(1)
                    if step == "mean":
                        for h in range(2):
                            pe.wait_ge(S["o_ready"], hd[h])
                            pe.matmul(aux[:, h, 0:n], ones, o_b[h][:, 0:n], start=True, stop=True)\
                              .then_inc(S["mean_psum"], 1)
                    if step == "var":
                        for h in range(2):
                            pe.wait_ge(S["osq_ready"], hd[h])
                            pe.matmul(aux[:, 2 + h, 0:n], ones, t_b[h][:, 0:n], start=True, stop=True)\
                              .then_inc(S["var_psum"], 1)

                def at(i, d, steps):
                    return {t: (lambda s=s: ret_heads(s, i, d)) for t, s in steps.items()}

                c0, g0 = C0[L["ret"]], G0[L["ret"]]
                RET_STEPS = [{1: "transpose", 4: "scores0"}, {1: "values0", 7: "values1"}, {2: "mean"}, {0: "var"}]

                def ret_round(i, heads):
                    for c in range(8):
                        g = c // 2
                        if c % 2 == 0:
                            bank_wait(i, 4, g0 + g)
                        hooks = at(i, -1, RET_STEPS[c]) if heads and c < 4 else {}
                        if c == 4:
                            def rotate_k():
                                pe.wait_ge(S["kvq_ready"], i * 3 + (3 * r0 + 1))
                                pe.wait_ge(S["rstd_ready"], n_stat[0])
                                rotate(k_b, 0)
                            hooks = {2: rotate_k}
                        if c == 1 and not heads:
                            hooks = {4: conv_stat}
                        chunk(i, 8, c0 + c, 512 if WINDOWS[g] in "kv" else n, norm_op, 8 * (c % 2), g % 2,
                              c % 2 == 0, c % 2 == 1, hooks)

                pe.wait_ge(S["norm_ready"], 8 * (layer + 1))
                ret_round(0, False)
                with pe.Fori(1, 4) as i:
                    ret_round(i, True)

                c0, g0 = C0[L["out"]], G0[L["out"]]

                def out_round(i, heads):
                    for c in range(4):
                        g, part = c % 2, c // 2
                        if part == 0:
                            bank_wait(i, 2, g0 + g)
                        if heads and c == 2:
                            ret_heads("mean", 4, -1)
                            ret_heads("var", 4, -1)
                            pe.wait_ge(S["ret_done"], HEADS * (layer + 1))
                        chunk(i, 4, c0 + c, n, mix_op, 8 * part, g, part == 0, part == 1,
                              at(4, -1, RET_STEPS[c]) if heads and c < 2 else {})

                pe.wait_ge(S["conv_done"], layer + 1)
                out_round(0, True)
                with pe.Fori(1, 4) as i:
                    out_round(i, False)

            pe.wait_ge(S["tile_sum"], 16 + 1)
            tile_stat(TOK)
            block_stat()

            def dt_project():
                pe.wait_ge(S["norm_ready"], 20)
                pe.wait_ge(S["rstd_ready"], n_stat[0])
                pe.wait_ge(S["dtw_lo"], 1)
                for t in range(KT):
                    wh, wl = (w[:, 32 * t:32 * t + 32] for w in (dtw_hi, dtw_lo))
                    pe.matmul(aux[0:32, 1, 0:TOK], wh, u_op[0][:, t, :], start=t == 0, stop=False)
                    pe.matmul(aux[0:32, 1, 0:TOK], wh, u_op[1][:, t, :], start=False, stop=False)
                    mm = pe.matmul(aux[0:32, 1, 0:TOK], wl, u_op[0][:, t, :], start=False, stop=t == KT - 1)
                mm.then_inc(S["dt_psum"], 1)

            def dt_transpose():
                pe.wait_ge(S["dt_ready"], 1)
                for n_, src in enumerate((dt_x, dt_a)):
                    for j in range(2):
                        at_ = 64 * n_ + 32 * j
                        mm = pe.transpose(aux[:, 2, at_:at_ + 32], src[:, j * P:(j + 1) * P], ident[0:32, 0:32])
                mm.then_inc(S["dt_psum_t"], 1)

            def dt_cumulate():
                pe.wait_ge(S["dt_t"], 2)
                pe.wait_ge(S["tri_ready"], 1)
                for j in range(2):
                    pe.matmul(aux[0:32, 3, 0:TOK], adt_t[:, 32 * j:32 * j + 32], tri[:, j * TOK:(j + 1) * TOK],
                              start=j == 0, stop=j == 1)
                for q in range(2):
                    for j in range(2):
                        mm = pe.matmul(aux[:, 3, TOK + 32 * q:TOK + 32 * q + 32],
                                       tri[:, j * TOK + q * P:j * TOK + (q + 1) * P], adt_t[:, 32 * j:32 * j + 32],
                                       start=j == 0, stop=j == 1)
                mm.then_inc(S["cum_psum"], 1)

            def att_heads(step, i, g):
                hd = [i * 4 + (2 * g + m + 1) for m in range(2)]

                def att_scores(m):
                    q_, k_ = att_qkv[0][:, m * TOK:(m + 1) * TOK], att_qkv[1][:, m * TOK:(m + 1) * TOK]
                    pe.matmul(aux[:, 0, 0:P], q_[:, 0:P], k_[:, 0:P], start=True, stop=True)
                    pe.matmul(aux[:, 0, P:P + TOK], q_[:, P:TOK], k_, start=True, stop=True)\
                      .then_inc(S["att_scores"], 1)

                def turn_p(m):
                    pe.wait_ge(S["att_p"], hd[m])
                    for j in range(3):
                        mm = pe.transpose(aux[:, 1, j * P:(j + 1) * P], att_s[m][:, j * P:(j + 1) * P], ident)
                    mm.then_inc(S["att_pt_psum"], 1)

                def att_values(m):
                    pe.wait_ge(S["att_pt"], hd[m])
                    wait_if(pe, S["att_done"], hd[m] - 1)
                    v0, v1 = (att_vt[:, m * TOK + j * P:m * TOK + (j + 1) * P] for j in range(2))
                    pe.matmul(aux[:, 3, 0:TOK], v0, att_pt[:, 0:TOK], start=True, stop=False)
                    pe.matmul(aux[:, 3, P:TOK], v1, att_pt[:, TOK:384], start=False, stop=True)\
                      .then_inc(S["att_o"], 1)

                if step == 0:
                    pe.wait_ge(S["att_qkv"], i * 6 + (3 * g + 3))
                    for m in range(2):
                        for j in range(2):
                            mm = pe.transpose(aux[:, 2, m * TOK + j * P:m * TOK + (j + 1) * P],
                                              att_qkv[2][:, m * TOK + j * P:m * TOK + (j + 1) * P], ident)
                    mm.then_inc(S["att_vt_psum"], 1)
                    att_scores(0)
                if step == 1:
                    turn_p(0)
                    att_scores(1)
                if step == 2:
                    pe.wait_ge(S["att_vt"], i * 2 + (g + 1))
                    att_values(0)
                    turn_p(1)
                if step == 3:
                    att_values(1)

            c0, g0 = C0["att"], G0["att"]

            def att_round(i, heads):
                for c in range(12):
                    sub, step = c // 6, c % 6
                    if c % 2 == 0:
                        bank_wait(i, 6, g0 + c // 2)
                    hooks = {1: lambda: att_heads(step, i, sub - 1)} if (heads or sub) and step < 4 else {}
                    if not heads and not sub:
                        hooks = {2: {0: dt_project}, 4: {0: dt_transpose}, 5: {2: dt_cumulate}}.get(step, {})
                    if not heads and c == 6:
                        pe.wait_ge(S["cum_ready"], 3)
                    chunk(i, 12, c0 + c, TOK, u_op, 8 * (c % 2), (c // 2) % 2, c % 2 == 0, c % 2 == 1, hooks,
                          normed(16, 1) if not heads and c < 2 else None)

            att_round(0, False)
            with pe.Fori(1, 4) as i:
                att_round(i, True)

            def ssd_heads(step, i, g):
                gr, b = i * 2 + g, g % 2

                def rows_out(r):
                    hd = i * 8 + (4 * g + r)
                    pe.wait_ge(S["row_ready"], hd + 1)
                    wait_if(pe, S["decay_ready"], hd * 2)
                    pe.matmul(aux[:, 2, 0:384], ones[0:SSM_HEADS, :], rows, start=True, stop=False)
                    pe.matmul(aux[:, 2, 0:P], ident_bf, causal_bf, start=False, stop=False)
                    pe.matmul(aux[:, 2, TOK:384], ident_bf, causal_bf, start=False, stop=True)\
                      .then_inc(S["row_psum"], 1)

                def y_out(r):
                    pe.wait_ge(S["pw_ready"], i * 8 + (4 * g + r + 1))
                    at_, m = (r % 2) * 64, r // 2
                    pe.matmul(aux[at_:at_ + 64, 3, m * TOK:(m + 1) * TOK], xt[:, m * P + at_:m * P + at_ + 64],
                              pw[r % 2][:, 0:TOK], start=True, stop=False)
                    pe.matmul(aux[at_:at_ + 64, 3, m * TOK + P:(m + 1) * TOK],
                              xt[:, TOK + m * P + at_:TOK + m * P + at_ + 64], pw[r % 2][:, TOK:384],
                              start=False, stop=True).then_inc(S["pw_used"], 1)

                if step == "gram":
                    pe.wait_ge(S["xbc_ready"], gr + 1)
                    for m in range(2):
                        for j in range(2):
                            mm = pe.transpose(aux[:, 0, j * TOK + m * P:j * TOK + (m + 1) * P],
                                              xbc[b][:, m, j * P:(j + 1) * P], ident)
                    mm.then_inc(S["xt_psum"], 1)
                    pe.matmul(aux[:, 1, 0:TOK], xbc[b][:, 2, 0:P], xbc[b][:, 3, :], start=True, stop=True)
                    pe.matmul(aux[:, 1, TOK:384], xbc[b][:, 2, P:TOK], xbc[b][:, 3, P:TOK], start=True, stop=True)\
                      .then_inc(S["gram_psum"], 1)
                if step == "rows0":
                    rows_out(0)
                if step == "rows1":
                    rows_out(1)
                if step == "y0":
                    pe.wait_ge(S["xt_ready"], gr + 1)
                    y_out(0)
                    rows_out(2)
                if step == "y1":
                    y_out(1)
                if step == "rows3":
                    rows_out(3)
                if step == "y2":
                    y_out(2)
                if step == "y3":
                    y_out(3)
                if step == "var":
                    pe.wait_ge(S["yg_sq"], gr + 1)
                    pe.matmul(aux[:, 0, 0:TOK], ones, yg_sq[:, 0, :], start=True, stop=False)
                    pe.matmul(aux[:, 0, 0:TOK], ones, yg_sq[:, 1, :], start=False, stop=True)\
                      .then_inc(S["yg_psum"], 1)

            SSD_STEPS = [{}, {6: "rows0"}, {4: "gram", 5: "rows1", 7: "y0"}, {2: "y1", 3: "rows3", 6: "y2"},
                         {0: "y3", 7: "var"}, {}]

            def ssd_at(i, g, steps):
                return {t: (lambda s=s: ssd_heads(s, i, g)) for t, s in steps.items()}

            c0, g0 = C0["ssd"], G0["ssd"]

            def ssd_round(i, heads):
                for c in range(12):
                    sub, step = c // 6, c % 6
                    if c % 2 == 0:
                        bank_wait(i, 6, g0 + c // 2)
                    if heads or sub:
                        hooks = ssd_at(i, sub - 1, SSD_STEPS[step])
                    else:
                        hooks = {1: lambda: att_heads(step, 4, -1)} if step < 4 else {}
                    if not heads and c == 6:
                        pe.wait_ge(S["att_done"], ATT_HEADS)
                    chunk(i, 12, c0 + c, TOK, u_op, 8 * (c % 2), (c // 2) % 2, c % 2 == 0, c % 2 == 1, hooks)

            ssd_round(0, False)
            with pe.Fori(1, 4) as i:
                ssd_round(i, True)

            c0, g0 = C0["mixout"], G0["mixout"]

            def mix_round(i, heads):
                for c in range(8):
                    ssm, g, part = c >= 4, (c // 2) % 2, c % 2
                    if c in (0, 2):
                        bank_wait(i, 2, g0 + g)
                    if heads and c == 4:
                        ssd_heads("y3", 4, -1)
                        ssd_heads("var", 4, -1)
                        pe.wait_ge(S["ssd_done"], SSM_GROUPS)
                    chunk(i, 8, c0 + c, TOK, mix2_op, (0 if ssm else KT) + 8 * part, g, not ssm and part == 0,
                          ssm and part == 1, ssd_at(4, -1, SSD_STEPS[c]) if heads and c < 4 else {})

            mix_round(0, True)
            with pe.Fori(1, 4) as i:
                mix_round(i, False)
            pe.wait_ge(S["tile_sum"], 24 + 1)
            tile_stat(TOK)
            block_stat()

            with pe.Fori(0, 16) as i:
                for c in range(4):
                    k, part = c // 2, c % 2
                    if part == 0:
                        bank_wait(i, 2, G0["up"] + k)
                    chunk(i, 4, C0["up"] + c, TOK, u_op, 8 * part, k, part == 0, part == 1,
                          ready=normed(20, 1) if k == 0 else None)

            with pe.Fori(0, 4) as i:
                for c in range(16):
                    k, part = c // 8, c % 8
                    if part == 0:
                        bank_wait(i, 2, G0["down"] + k)
                    if k == 0:
                        pe.wait_ge(S["hid_ready"], 4 * (part + 1))
                    chunk(i, 16, C0["down"] + c, TOK, hid_op, 8 * part, k, part == 0, part == 7)
            pe.wait_ge(S["tile_sum"], 32 + 1)
            tile_stat(TOK)

        @block.vector
        def _(dve):
            chain = Chain(dve, dve_chain)
            link = chain.link
            stt = dve.scalar_tensor_tensor

            def split_lo(i, per, c):
                slot = c % SLOTS
                dve.wait_ge(hi_ready, i * per + (c + 1))
                stt(w_lo[:, slot, :], raw[:, slot, :], W_SCALE, w_hi[:, slot, :], ALU.mult, ALU.subtract)\
                    .then_inc(lo_ready, 1)

            def chunk_wait(i, per, c):
                dve.wait_ge(chunk_free, i * per + (c + 1 + SLOTS))

            def silu(z, e, s):
                link(stt(e, z, 0.0, e, ALU.min, ALU.mult))
                link(stt(z, z, 0.0, e, ALU.max, ALU.add))
                return dve.tensor_tensor(z, z, s, ALU.mult)

            def over(v, reps):
                return v.rearrange("p (a n) -> p a n", a=1).to_broadcast([P, reps, v.shape[-1]])

            for name in FREE_AT_FIRST:
                dve.sem_inc(S[name], 1)
            dve.memset(eps[:, :], EPS).then_inc(dve_chain, 1)
            chain.k += 1
            dve.wait_ge(S["c_sigmoid"], 1)
            cc = par[:, PCOLS["c"]:PCOLS["c"] + 32]
            link(stt(silu_c, cc, 0.0, tmp[:, 0:32], ALU.min, ALU.mult))
            link(stt(silu_c, cc, 0.0, silu_c, ALU.max, ALU.add))
            dve.tensor_tensor(silu_c, silu_c, tmp[:, 32:64], ALU.mult).then_inc(S["c_silu"], 1)
            for c in range(AHEAD):
                split_lo(0, 0, c)
            dve.wait_ge(S["c_silu"], 1)
            dve.wait_ge(S["c_hi"], 1)
            stt(cvec[:, :, :, 1], c_silu, A_SCALE, cvec[:, :, :, 0], ALU.mult, ALU.subtract).then_inc(S["c_lo"], 1)

            def mod_out(src, i, per, tile):
                dst = modraw[:, bass.ds(i * (2 * per) + 2 * tile, 4)].rearrange("p (m s) -> p m s", m=2)
                return dve.tensor_reduce(dst, src.rearrange("p m (s h) -> p m s h", h=2), AX.X, ALU.add)

            link(dve.memset(tile_total, 0.0))
            with dve.Fori(0, 8) as i:
                chain.enter(i, 1)
                for c in range(4):
                    split_lo(i, 4, c + AHEAD)
                    if c % 2:
                        k = c // 2
                        chunk_wait(i, 4, c)
                        mod_out(proj[:, 2 * k:2 * k + 2, 0:4], i, 4, 2 * k).then_inc(bank_free[k], 1)
                    if c == 2:
                        dve.wait_ge(S["first_squares"], i + 1)
                        dve.wait_ge(S["first_sum"], i + 1)
                        link(dve.tensor_tensor(tile_total, tile_total, first_squares[:, 0, :], ALU.add))
                        dve.tensor_tensor(tile_total, tile_total, first_squares[:, 1, :], ALU.add)\
                           .then_inc(S["first_sum"], 1)
            chain.leave(8)

            def mod_view(layer, t0, t1):
                return modraw[:, 96 * layer + 2 * t0:96 * layer + 2 * t1].rearrange("p (t s) -> p t s", s=2)

            def per_tile(name, t0, t1):
                c0 = PCOLS[name]
                return par[:, c0 + t0:c0 + t1].rearrange("p (t a) -> p t a", a=1).to_broadcast([P, t1 - t0, 2])

            def make_affine(layer):
                m = mod_view(layer, 0, 2 * KT)
                link(stt(m, m, UNSCALE, per_tile("b_mod", 48 * layer, 48 * layer + 2 * KT), ALU.mult, ALU.add))
                link(stt(affine[:, 0, :, :], mod_view(layer, KT, 2 * KT), 1.0,
                         per_tile("norm_w", KT * layer, KT * (layer + 1)), ALU.add, ALU.mult))
                link(dve.tensor_scalar(affine[:, 0, :, :], affine[:, 0, :, :], A_SCALE, None, ALU.mult))
                link(dve.tensor_scalar(affine[:, 1, :, :], mod_view(layer, 0, KT), A_SCALE, None, ALU.mult))

            def make_gates():
                for layer in range(2):
                    g = gates[:, 32 * layer:32 * layer + 32].rearrange("p (t s) -> p t s", s=2)
                    link(stt(g, mod_view(layer, 2 * KT, 3 * KT), UNSCALE,
                             per_tile("b_mod", 48 * layer + 2 * KT, 48 * layer + 3 * KT), ALU.mult, ALU.add))
                    link(dve.tensor_scalar(g, g, UNSCALE, None, ALU.mult))

            n_stat, n_blocks, n_updated, n_squares = [0], [0], [0], [0]

            def rstd_wait():
                n_stat[0] += 1
                dve.wait_ge(S["rstd_ready"], n_stat[0])

            def norm_split(blocks, scale_shift):
                def lo_of(block, count):
                    _, dst, d_hi, d_lo, _, _ = block
                    dve.wait_ge(S["scaled"], count)
                    dve.wait_ge(S["norm_hi"], count)
                    dve.tensor_tensor(d_lo, dst, d_hi, ALU.subtract).then_inc(S["norm_ready"], 1)

                for n_, (src, dst, d_hi, d_lo, t0_, s) in enumerate(blocks):
                    link(dve.tensor_tensor(dst, src, over(rstd[:, s * TOK:(s + 1) * TOK], 4), ALU.mult))
                    for t in range(4):
                        ins = scale_shift(dst[:, t, :], t0_ + t, s)
                    ins.then_inc(S["scaled"], 1)
                    n_blocks[0] += 1
                    if n_:
                        lo_of(blocks[n_ - 1], n_blocks[0] - 1)
                lo_of(blocks[-1], n_blocks[0])

            def tiles4(op, b, s=0):
                return op[:, 4 * b:4 * b + 4, s * TOK:(s + 1) * TOK]

            def modulate(v, t, s):
                return dve.tensor_scalar(v, v, affine[:, 0, t, s:s + 1], affine[:, 1, t, s:s + 1], ALU.mult, ALU.add)

            def weigh(name):
                return lambda v, t, s: dve.tensor_scalar(v, v, col(name, t), A_SCALE, ALU.mult, ALU.mult)

            def sum_tiles(i, g, n):
                dve.wait_ge(S["tile_sq"], i * 2 + (g + 1))
                dve.wait_ge(S["tile_sum"], i * 2 + (g + 1))
                link(dve.tensor_tensor(tile_total[:, 0:n], tile_total[:, 0:n], tile_squares[:, 0, 0:n], ALU.add))
                dve.tensor_tensor(tile_total[:, 0:n], tile_total[:, 0:n], tile_squares[:, 1, 0:n], ALU.add)\
                   .then_inc(S["tile_sum"], 1)

            for layer, L in enumerate(LAYERS):
                n, r0, win, s_n = L["n"], 4 * layer, L["window"], L["n"] // TOK
                if layer == 0:
                    for half in range(2):
                        dve.wait_ge(bank_free[half], 1 + G0[L["conv"]] // 2)
                make_affine(layer)
                rstd_wait()
                norm_split([(tiles4((x3, ctx3)[s], b), ctx_stage(b) if s else tiles4(stage16, b),
                             tiles4(norm_op[0], b, s), tiles4(norm_op[1], b, s), 4 * b, s)
                            for s, b in NORM_ORDER[layer]], modulate)

                dve.memset(pad[:, :, :, 0:1], 0.0)
                dve.memset(pad[:, :, :, 257:258], 0.0)
                link(dve.memset(conv_sum, 0.0))
                per, c0, g0 = 4 * win, C0[L["conv"]], G0[L["conv"]]
                h_t, z_t = pair(za, 0, 512), pair(za, 1024, 512)
                e_t, s_t = pair(zb, 0, 512), pair(zb, 1024, 512)
                with dve.Fori(0, 4) as i:
                    chain.enter(i, 3 + 1 + 3)
                    for c in range(per):
                        split_lo(i, per, c0 + c + AHEAD)
                        w = c // win
                        bank = banks(w % 2, n)
                        if c % win > 3:
                            u = c % win - 4
                            chunk_wait(i, per, c0 + c)
                            per_i, tile = ((8, 48 + 4 * w), (8, 48 + 4 * w), (4, 32), (4, 80))[w]
                            mod_out(aux[:, 2 * u:2 * u + 2, 0:4], i, per_i, tile + 2 * u).then_inc(S["mods_read"], 1)
                        if c % win != win // 2:
                            continue
                        if w == 1:
                            chunk_wait(i, per, c0 + c)
                            dve.wait_ge(S["conv_h"], i + (r0 + 1))
                            for m in range(2):
                                ins = stt(pad[:, m, 0:s_n, 1:257], bank[:, m, :].rearrange("p (s n) -> p s n", n=TOK),
                                          UNSCALE, h_t[:, m, 0:n].rearrange("p (s n) -> p s n", n=TOK),
                                          ALU.mult, ALU.mult)
                            ins.then_inc(S["conv_in"], 1)
                            dve.wait_ge(S["conv_in"], i + (r0 + 1) + 1)
                            dve.sem_inc(bank_free[1], 1)
                            for tap in range(3):
                                for m in range(2):
                                    wt = cols("conv_w", i, 2, (3 * layer + tap) * 8 + m)
                                    src = pad[:, m, 0:s_n, tap:tap + TOK]
                                    dst = conv_t[:, m * 512:m * 512 + n].rearrange("p (s n) -> p s n", n=TOK)
                                    if tap == 0:
                                        ins = dve.tensor_scalar(dst, src, wt, None, ALU.mult)
                                    else:
                                        ins = stt(dst, src, wt, dst, ALU.mult, ALU.add)
                                link(ins)
                        if w == 2:
                            chunk_wait(i, per, c0 + c)
                            stt(stage8[:, bass.ds(i * 2, 2), 0:n], bank, UNSCALE, pair(conv_t, 0, 512)[:, :, 0:n],
                                ALU.mult, ALU.mult).then_inc(S["conv_y"], 1)
                            dve.wait_ge(S["conv_y"], i + (r0 + 1))
                            dve.sem_inc(bank_free[0], 1)
                        if w == 3:
                            dve.wait_ge(S["conv_sq"], i + (r0 + 1))
                            sq = pair(conv_sq, 0, 512)
                            link(dve.tensor_tensor(conv_sum[:, 0:n], conv_sum[:, 0:n], sq[:, 0, 0:n], ALU.add))
                            dve.tensor_tensor(conv_sum[:, 0:n], conv_sum[:, 0:n], sq[:, 1, 0:n], ALU.add)\
                               .then_inc(S["conv_sum"], 1)
                            dve.wait_ge(S["conv_sum"], i + (r0 + 1) + 1)
                            dve.wait_ge(S["conv_z"], i + (r0 + 1))
                            link(silu(z_t[:, :, 0:n], e_t[:, :, 0:n], s_t[:, :, 0:n]))
                            for m in range(2):
                                y = stage8[:, bass.ds(i * 2 + m, 1), 0:n]
                                ins = stt(y, y, cols("conv_norm_w", i, 2, 8 * layer + m), z_t[:, m:m + 1, 0:n],
                                          ALU.mult, ALU.mult)
                            ins.then_inc(S["conv_g"], 1)
                chain.leave(4)
                dve.wait_ge(S["conv_g"], r0 + 4 + 1)
                rstd_wait()
                dve.tensor_tensor(stage8[:, :, 0:n], stage8[:, :, 0:n], over(rstd[:, 0:n], 8), ALU.mult)\
                   .then_inc(S["conv_scaled"], 1)
                dve.wait_ge(S["conv_scaled"], layer + 1)
                dve.wait_ge(S["conv_hi"], layer + 1)
                stt(mix_op[1][:, 0:8, 0:n], stage8[:, :, 0:n], A_SCALE, mix_op[0][:, 0:8, 0:n],
                    ALU.mult, ALU.subtract).then_inc(S["conv_done"], 1)

                def rope(i, buf, bank, t, count):
                    dve.wait_ge(S["rot_done"], count)
                    v = pair(buf, 0, 512)[:, :, 0:TOK]
                    dve.tensor_tensor(t, aux[:, bank, :].rearrange("p (m n) -> p m n", m=2), over(sin, 2), ALU.mult)
                    link(dve.tensor_tensor(v, v, over(cos, 2), ALU.mult))
                    dve.tensor_tensor(v, v, t, ALU.add).then_inc(S["roped"], 1)

                def ret_heads(step, i, d):
                    hd = [i * 2 + (2 * (r0 + d) + h + 1) for h in range(2)]

                    def weights(h):
                        dve.wait_ge(S["mask_exp"], i * 8 + (8 * (r0 + d) + 4 * h + 4))
                        dve.tensor_tensor(mask_x, mask_x, is_ge, ALU.mult)
                        dve.tensor_tensor(mask_c, mask_c, t_b[1], ALU.add)
                        link(dve.tensor_tensor(t_b[0], t_b[0], is_le, ALU.mult))
                        link(dve.tensor_tensor(mask_x, mask_x, t_b[0], ALU.add))
                        dve.wait_ge(S["scores_done"], hd[h])
                        dve.tensor_tensor(p_b[:, 0, :], aux[:, 0, :], mask_x, ALU.mult)
                        if n == 512:
                            dve.tensor_tensor(p_b[:, 2, :], aux[:, 2, :], mask_x, ALU.mult)
                        dve.tensor_tensor(p_b[:, 1, :], aux[:, 1, :], mask_c, ALU.mult).then_inc(S["p_ready"], 1)

                    if step == 0:
                        dve.wait_ge(S["z_silu"], i + (r0 + d + 1))
                        rope(i, q_b, 1, pair(o_b[0], 0, TOK), i * 2 + (2 * (r0 + d) + 2))
                        weights(0)
                    if step == 1:
                        weights(1)
                    if step == 2:
                        for h in range(2):
                            dve.wait_ge(S["mean_psum"], hd[h])
                            stt(o_b[h][:, 0:n], aux[:, h, 0:n], -1.0 / P, o_b[h][:, 0:n], ALU.mult, ALU.add)\
                                .then_inc(S["centered"], 1)
                    if step == 3:
                        for h in range(2):
                            dve.wait_ge(S["centered"], hd[h])
                            dve.wait_ge(S["orstd_ready"], hd[h])
                            dve.wait_ge(S["osq_ready"], hd[h])
                            link(stt(o_b[h][:, 0:n], o_b[h][:, 0:n], cols("ret_norm_w", i, 2, 8 * layer + 2 * d + h),
                                     orstd[h][:, 0:n], ALU.mult, ALU.mult))
                            dve.tensor_tensor(o_b[h][:, 0:n], o_b[h][:, 0:n], z_b[:, h * 512:h * 512 + n], ALU.mult)\
                               .then_inc(S["y_ready"], 1)
                        for h in range(2):
                            dve.wait_ge(S["y_ready"], hd[h])
                            dve.wait_ge(S["y_hi"], hd[h])
                            tile = bass.ds(i * 2 + (8 + 2 * d + h), 1)
                            stt(mix_op[1][:, tile, 0:n], o_b[h][:, 0:n].rearrange("p (a n) -> p a n", a=1), A_SCALE,
                                mix_op[0][:, tile, 0:n], ALU.mult, ALU.subtract).then_inc(S["ret_done"], 1)

                c0 = C0[L["ret"]]

                def ret_round(i, heads):
                    for c in range(8):
                        split_lo(i, 8, c0 + c + AHEAD)
                        if heads and c < 4:
                            ret_heads(c, i, -1)
                        if c == 5:
                            rope(i, k_b, 0, pair(t_b[1], 0, TOK), i * 2 + (2 * r0 + 1))
                        if c == 6:
                            dve.wait_ge(S["z_sigmoid"], i + (r0 + 1))
                            silu(*(pair(b, 0, 512)[:, :, 0:n] for b in (z_b, e_b, s_b))).then_inc(S["z_silu"], 1)

                ret_round(0, False)
                with dve.Fori(1, 4) as i:
                    chain.enter(i, 1 + 2 + 1 + 2 + 2 + 2, 1)
                    ret_round(i, True)
                chain.leave(4)

                if layer == 0:
                    make_gates()
                c0 = C0[L["out"]]

                def out_round(i, heads):
                    for c in range(4):
                        split_lo(i, 4, c0 + c + AHEAD)
                        if heads and c < 3:
                            for step in ((0,), (1,), (2, 3))[c]:
                                ret_heads(step, 4, -1)
                            if c == 2:
                                link(dve.memset(tile_total, 0.0))
                        if c < 2:
                            continue
                        k = c - 2
                        chunk_wait(i, 4, c0 + c)
                        for s in range(s_n):
                            for m in range(2):
                                res = (x3, ctx3)[s][:, bass.ds(i * 4 + (2 * k + m), 1), :]
                                gate = gates[:, bass.ds(i * 8 + (32 * layer + 2 * (2 * k + m) + s), 1)]
                                ins = stt(res, proj[:, 2 * k + m:2 * k + m + 1, s * TOK:(s + 1) * TOK], gate, res,
                                          ALU.mult, ALU.add)
                        ins.then_inc(S["res_part"], 1)
                        dve.wait_ge(S["res_part"], i * 2 + (8 * layer + k + 1))
                        dve.sem_inc(bank_free[k], 1)
                        sum_tiles(i, 8 * layer + k, n)

                out_round(0, True)
                with dve.Fori(1, 4) as i:
                    chain.enter(i, 2, 1)
                    out_round(i, False)
                chain.leave(4)

            def updated_blocks(update, squares):
                def sum_block(b):
                    n_squares[0] += 1
                    dve.wait_ge(S["squares_ready"], n_squares[0])
                    dve.tensor_reduce(block_sums[b], tiles4(sq256, b).rearrange("p t n -> p n t"), AX.X, ALU.add)\
                       .then_inc(S["sums_ready"], 1)

                for b in range(4):
                    update(b).then_inc(S["x_block"], 1)
                    n_updated[0] += 1
                    if b and squares:
                        sum_block(b - 1)
                if squares:
                    sum_block(3)
                dve.wait_ge(S["x_block"], n_updated[0])

            rstd_wait()

            def final_norm(b):
                link(dve.tensor_tensor(tiles4(x3, b), tiles4(x3, b), over(rstd[:, 0:TOK], 4), ALU.mult))
                for t in range(4 * b, 4 * b + 4):
                    ins = dve.tensor_scalar(x3[:, t, :], x3[:, t, :], col("final_norm_w", t), None, ALU.mult)
                return ins

            def norm_x(name):
                rstd_wait()
                norm_split([(tiles4(x3, b), tiles4(stage16, b), tiles4(u_op[0], b), tiles4(u_op[1], b), 4 * b, 0)
                            for b in range(4)], weigh(name))

            updated_blocks(final_norm, True)
            norm_x("mix_pre")

            def step_weights():
                dve.wait_ge(S["dtw_hi"], 1)
                stt(dtw_lo, tmp[:, 0:512], W_SCALE, dtw_hi, ALU.mult, ALU.subtract).then_inc(S["dtw_lo"], 1)

            def step_sizes():
                dve.wait_ge(S["dt_log"], 1)
                link(dve.tensor_scalar(dt_um, dt_e, 1.0, None, ALU.add))
                link(dve.tensor_scalar(dt_um, dt_um, -1.0, None, ALU.add))
                link(dve.tensor_scalar(dt_eq, dt_um, 0.0, None, ALU.is_equal))
                link(dve.tensor_tensor(dt_um, dt_um, dt_eq, ALU.add))
                link(dve.reciprocal(dt_um, dt_um))
                link(dve.tensor_tensor(dt_um, dt_um, dt_e, ALU.mult))
                link(dve.tensor_tensor(dt_l, dt_l, dt_um, ALU.mult))
                link(dve.tensor_tensor(dt_eq, dt_eq, dt_e, ALU.mult))
                link(dve.tensor_tensor(dt_l, dt_l, dt_eq, ALU.add))
                link(stt(dt_x, dt_x, 0.0, dt_l, ALU.max, ALU.add))
                dve.wait_ge(S["a_ready"], 1)
                dve.tensor_scalar(dt_a, dt_x, hcol[:, 2:3], -1.0, ALU.mult, ALU.mult).then_inc(S["dt_ready"], 1)

            def att_heads(step, i, g):
                m = step % 2
                hd = i * 4 + (2 * g + m + 1)
                if step < 2:
                    dve.wait_ge(S["att_scores"], hd)
                    link(dve.tensor_tensor(att_s[m], aux[:, 0, 0:384], att_log, ALU.add))
                    dve.tensor_reduce(att_m[m][:, 0:1], att_s[m][:, 0:128], AX.X, ALU.max, negate=True)
                    dve.tensor_reduce(att_m[m][:, 1:2], att_s[m][:, 128:384], AX.X, ALU.max, negate=True)\
                       .then_inc(S["att_max"], 1)
                    dve.wait_ge(S["att_exp"], i * 8 + (4 * g + 2 * m + 2))
                    link(dve.reciprocal(att_r[m], att_sum[m]))
                    dve.tensor_scalar(att_s[m][:, 0:128], att_s[m][:, 0:128], att_r[m][:, 0:1], None, ALU.mult)
                    dve.tensor_scalar(att_s[m][:, 128:384], att_s[m][:, 128:384], att_r[m][:, 1:2], None, ALU.mult)\
                       .then_inc(S["att_p"], 1)
                else:
                    dve.wait_ge(S["att_hi"], hd)
                    tile = bass.ds(i * 4 + (KT + 2 * g + m), 1)
                    stt(mix2_op[1][:, tile, :], aux[:, 3:4, 0:TOK], A_SCALE, mix2_op[0][:, tile, :],
                        ALU.mult, ALU.subtract).then_inc(S["att_done"], 1)

            def att_round(i, heads):
                for c in range(12):
                    split_lo(i, 12, C0["att"] + c + AHEAD)
                    sub, step = c // 6, c % 6
                    if (heads or sub) and step < 4:
                        att_heads(step, i, sub - 1)
                    if not heads and c in (0, 3):
                        (step_sizes if c else step_weights)()
                    if not heads and c == 5:
                        dve.wait_ge(att_in, 16)
                        dve.wait_ge(S["cum_ready"], 3)

            att_round(0, False)
            with dve.Fori(1, 4) as i:
                chain.enter(i, 2 * 2 * 2, 1)
                att_round(i, True)
            chain.leave(4)

            def conv(q, i, g):
                gr, b = i * 2 + g, g % 2
                dve.wait_ge(S["xbc_pad"], gr * 2 + (q + 1))
                for tap in range(4):
                    for m in range(2):
                        per_i, tile = (4, 2 * g + m) if q == 0 else (2, KT + 8 * m + g)
                        dst, src = xbc[b][:, 2 * q + m, :], pad2[:, 2 * q + m, tap:tap + TOK]
                        w = cols("conv_w2", i, per_i, 32 * tap + tile)
                        if tap == 0:
                            ins = dve.tensor_scalar(dst, src, w, cols("conv_b2", i, per_i, tile), ALU.mult, ALU.add)
                        else:
                            ins = stt(dst, src, w, dst, ALU.mult, ALU.add)
                    if tap < 3:
                        link(ins)
                ins.then_inc(S["xbc_conv"], 1)

            def conv_silu(i, g):
                gr, b = i * 2 + g, g % 2
                dve.wait_ge(S["xbc_conv"], gr * 2 + 2)
                dve.wait_ge(S["xbc_sigmoid"], gr + 1)
                silu(xbc[b], xbc_e, xbc_s).then_inc(S["xbc_ready"], 1)

            def ssd_heads(step, i, g):
                gr, b = i * 2 + g, g % 2

                def row(r):
                    hd = i * 8 + (4 * g + r)
                    wait_if(dve, S["row_psum"], hd)
                    dve.tensor_scalar(rows, acs, ident[0:SSM_HEADS, bass.ds(hd, 1)], None, ALU.mult)\
                       .then_inc(S["row_ready"], 1)

                def weights(r):
                    hd = i * 8 + (4 * g + r)
                    dve.wait_ge(S["decay_ready"], i * 16 + 2 * (4 * g + r + 1))
                    wait_if(dve, S["pw_used"], hd - 1)
                    stt(pw[r % 2][:, 0:TOK], aux[:, 1, 0:TOK], dt_t[:, bass.ds(hd, 1)], decay_w[r % 2][:, 0:TOK],
                        ALU.mult, ALU.mult)
                    stt(pw[r % 2][:, TOK:384], aux[:, 1, TOK:384], dt_t[:, bass.ds(hd + 32, 1)],
                        decay_w[r % 2][:, TOK:384], ALU.mult, ALU.mult).then_inc(S["pw_ready"], 1)

                if step == 0:
                    row(0)
                if step == 2:
                    row(1)
                    dve.wait_ge(S["gram_psum"], gr + 1)
                    weights(0)
                    row(2)
                    weights(1)
                    row(3)
                if step == 3:
                    weights(2)
                    weights(3)
                    dve.wait_ge(S["pw_used"], i * 8 + (4 * g + 4))
                    dve.wait_ge(S["xbc_ready"], gr + 1)
                    for m in range(2):
                        ins = stt(yg[:, m, :], xbc[b][:, m, :], dsk[:, bass.ds(i * 4 + (2 * g + m), 1)],
                                  aux[:, 3, m * TOK:(m + 1) * TOK], ALU.mult, ALU.add)
                    link(ins)
                    dve.wait_ge(S["zs_ready"], gr + 1)
                    dve.tensor_tensor(yg, yg, zs[b], ALU.mult).then_inc(S["yg_ready"], 1)
                if step == 5:
                    dve.wait_ge(S["yg_ready"], gr + 1)
                    dve.wait_ge(S["yg_rstd"], gr + 1)
                    for m in range(2):
                        ins = stt(yg[:, m, :], yg[:, m, :], cols("ssm_norm_w", i, 4, 2 * g + m), rstd[:, 0:TOK],
                                  ALU.mult, ALU.mult)
                    ins.then_inc(S["yg_norm"], 1)
                if step == 6:
                    dve.wait_ge(S["yg_norm"], gr + 1)
                    dve.wait_ge(S["yg_hi"], gr + 1)
                    tiles = bass.ds(i * 4 + 2 * g, 2)
                    stt(mix2_op[1][:, tiles, :], yg, A_SCALE, mix2_op[0][:, tiles, :], ALU.mult, ALU.subtract)\
                        .then_inc(S["ssd_done"], 1)

            def ssd_round(i, heads):
                for c in range(12):
                    sub, step = c // 6, c % 6
                    if heads or sub:
                        ssd_heads(step, i, sub - 1)
                        if step == 0:
                            conv(1, i, sub - 1)
                    if step == 4:
                        dve.wait_ge(S["zs_sigmoid"], i * 2 + (sub + 1))
                        silu(zs[sub], zs_e, zs_s).then_inc(S["zs_ready"], 1)
                        conv(0, i, sub)
                    split_lo(i, 12, C0["ssd"] + c + AHEAD)
                    if heads or sub:
                        if step == 0:
                            conv_silu(i, sub - 1)
                        if step == 5:
                            ssd_heads(6, i, sub - 1)
                    elif step < 4:
                        att_heads(step, 4, -1)

            link(dve.memset(pad2[:, :, 0:3], 0.0))
            ssd_round(0, False)
            with dve.Fori(1, 4) as i:
                chain.enter(i, 2 * (2 * 3 + 2 + 2 + 1), 1)
                ssd_round(i, True)
            chain.leave(4)

            def sum_stage(name, per, ends, tail):
                first = {"mixout": 16, "down": 24}[name]
                for i, last in ((0, False), (None, False), (3, True)):
                    if i is None:
                        with dve.Fori(1, 3) as i:
                            chain.enter(i, 2 * 1, 1)
                            one_round(i, name, per, ends, first, tail, last)
                        chain.leave(3)
                    else:
                        one_round(i, name, per, ends, first, tail, last)

            def one_round(i, name, per, ends, first, tail, last):
                for c in range(per):
                    if not (name == "down" and last and c + AHEAD >= per):
                        split_lo(i, per, C0[name] + c + AHEAD)
                    if tail and isinstance(i, int) and i == 0 and c < 4:
                        if c == 0:
                            conv(1, 4, -1)
                            conv_silu(4, -1)
                        for step in ((0,), (), (2,), (3, 5, 6))[c]:
                            ssd_heads(step, 4, -1)
                    if isinstance(i, int) and i == 0 and c == 4:
                        link(dve.memset(tile_total, 0.0))
                    if c in ends:
                        sum_tiles(i, first + ends.index(c), TOK)

            sum_stage("mixout", 8, (5, 7), True)

            def add_normed(name):
                rstd_wait()
                dve.wait_ge(S["stage_ready"], 8 if name == "mix_post" else 16)

                def update(b):
                    part = tiles4(stage16, b)
                    link(dve.tensor_tensor(part, part, over(rstd[:, 0:TOK], 4), ALU.mult))
                    for t in range(4 * b, 4 * b + 4):
                        ins = stt(x3[:, t, :], stage16[:, t, :], col(name, t), x3[:, t, :], ALU.mult, ALU.add)
                    return ins
                return update

            updated_blocks(add_normed("mix_post"), True)
            norm_x("mlp_pre")

            with dve.Fori(0, 16) as i:
                for c in range(4):
                    split_lo(i, 4, C0["up"] + c + AHEAD)
                    if c % 2 == 0:
                        continue
                    k = c // 2
                    chunk_wait(i, 4, C0["up"] + c)
                    dve.tensor_scalar(pair(tmp, 512 * k, TOK), banks(k, TOK), 0.0, UNSCALE, ALU.max, ALU.mult)\
                       .then_inc(S["relu_ready"], 1)
                    dve.wait_ge(S["relu_ready"], i * 2 + (k + 1))
                    dve.sem_inc(bank_free[k], 1)
                    dve.wait_ge(S["hid_hi"], i * 4 + (2 * k + 2))
                    tiles = bass.ds(i * 4 + 2 * k, 2)
                    dve.tensor_tensor(hid_op[1][:, tiles, :], pair(tmp, 1024 + 512 * k, TOK), hid_op[0][:, tiles, :],
                                      ALU.subtract).then_inc(S["hid_ready"], 1)

            sum_stage("down", 16, (7, 15), False)
            updated_blocks(add_normed("mlp_post"), False)


def constants():
    part = np.arange(P)
    ident = np.eye(P, dtype=np.float32)
    quarter = P // 4
    rot = np.zeros((P, P), np.float32)
    first = (part // quarter) % 2 == 0
    rot[part[first] + quarter, part[first]] = -1.0
    rot[part[~first] - quarter, part[~first]] = 1.0
    inv = (np.float32(10000.0) ** (-np.arange(quarter, dtype=np.float32) / np.float32(quarter))).astype(np.float32)
    tok = np.arange(TOK)
    pos = np.where(part[:, None] < P // 2, tok // 64, tok % 64).astype(np.float32)
    ang = pos * inv[part % quarter][:, None]
    i, j = tok[:, None], tok[None, :]
    seen = sum(((j <= i) & (i - j <= w) & ((i - j) % d == 0)).astype(np.int64)
               for w, d in ((128, 1), (512, 4), (2048, 16)))
    log = np.where(seen > 0, np.log(np.maximum(seen, 1)), -1e30).astype(np.float32)
    f32 = np.concatenate([ident, np.ones((P, P), np.float32), rot, np.cos(ang), np.sin(ang),
                          log[0:P, 0:P], log[P:, :]], axis=1).astype(np.float32)
    diff = (tok[None, None, :] - (part[:, None] + P * np.arange(2)[None, :])[:, :, None]).reshape(P, 512)
    causal = np.where(part[None, :] >= part[:, None], 0.0, -1e30)
    bf = np.concatenate([diff, diff >= 0, np.maximum(diff, 0), np.maximum(-diff, 0), diff <= 0, ident, causal],
                        axis=1)
    return f32, bf.astype(mybir.dt.np(BF16))


def kernel(**inputs):
    import concourse.bacc as _bacc
    from concourse.bass_utils import run_bass_kernel_spmd as _run

    a = {k: np.asarray(v) for k, v in inputs.items()}

    def tiles(v):
        return np.ascontiguousarray(v.reshape(-1, P).T)

    def chunked(w, columns):
        w = w[:, columns] if columns is not None else w
        k, m = w.shape
        return w.reshape(k // (P * CHUNK_K), CHUNK_K, P, m // WCOL, WCOL).transpose(3, 0, 2, 1, 4)\
            .reshape(-1, P, CHUNK_K * WCOL)

    w_mod, w_in, w_in2 = a["w_mod"], a["w_in"], a["w_in_2"][0]
    mod = [chunked(w_mod[l], None) for l in range(2)]
    blocks = [mod[0][0:32]]
    for l in range(2):
        h, b, c, z, q, k, v, rz = (chunked(w_in[l][:, 1024 * n:1024 * (n + 1)], None).reshape(4, 2, P, -1)
                                   for n in range(8))
        conv = np.stack([h, c, b, z], axis=1)
        if l == 0:
            scale_shift = mod[1][0:32].reshape(4, 2, 2, 2, P, -1)
            gate = np.stack([m[32:48].reshape(4, 2, 2, P, -1) for m in mod], axis=1)
            units = np.concatenate([scale_shift, gate], axis=1)
            conv = np.concatenate([conv[:, :, None], units], axis=2).swapaxes(2, 3)
        ret = np.stack([k, v, rz, q], axis=1)
        blocks += [conv.reshape(-1, P, CHUNK_K * WCOL), ret.reshape(-1, P, CHUNK_K * WCOL)]
        blocks.append(chunked(a["w_out"][l], None).reshape(4, 2, 2, P, -1).swapaxes(1, 2)
                      .reshape(-1, P, CHUNK_K * WCOL))
    base = D + 2 * D
    q0 = base + SSM_HEADS
    qkv = {n: chunked(w_in2[:, q0 + D * j:q0 + D * (j + 1)], None) for j, n in enumerate("qkv")}
    blocks.append(np.stack([m.reshape(8, 2, P, -1) for m in qkv.values()], axis=1).reshape(-1, P, CHUNK_K * WCOL))
    n_state = SSM_GROUPS * P
    bc = np.stack([w_in2[:, 2 * D:2 * D + n_state].reshape(D, SSM_GROUPS, P),
                   w_in2[:, 2 * D + n_state:2 * D + 2 * n_state].reshape(D, SSM_GROUPS, P)], axis=2)
    ssd = [chunked(w, None).reshape(8, 2, P, -1)
           for w in (w_in2[:, 0:D], w_in2[:, D:2 * D], bc.reshape(D, 2 * n_state))]
    blocks.append(np.stack(ssd, axis=1).reshape(-1, P, CHUNK_K * WCOL))
    blocks.append(chunked(a["w_out_2"][0], None).reshape(4, 2, 2, 2, P, -1)[:, :, ::-1].swapaxes(1, 2)
                  .reshape(-1, P, CHUNK_K * WCOL))
    blocks += [chunked(a[n][0], None) for n in ("w_up_2", "w_down_2")]
    stream = np.concatenate(blocks, axis=0)
    assert stream.shape == (N_CHUNKS, P, CHUNK_K * WCOL), stream.shape

    order = ("norm_w", "b_mod", "conv_w", "conv_norm_w", "ret_norm_w", "final_norm_w", "norm_mix_pre_2",
             "ssm_norm_w_2", "norm_mix_post_2", "norm_mlp_pre_2", "norm_mlp_post_2", "conv_w_2", "conv_b_2",
             "c", "c_ctx")
    params = np.concatenate([tiles(a[n]) for n in order], axis=1)
    assert params.shape == (P, N_PCOLS)
    heads_row = np.concatenate([a["ret_decay_f"].reshape(-1), a["ret_decay_b"].reshape(-1)])
    ssm_cols = np.stack([a["dt_bias_2"][0], a["a_log_2"][0]], axis=1)
    dskip = np.repeat(a["d_skip_2"][0].reshape(KT, 2).T, 64, axis=0)
    dt_w = w_in2[:, base:q0].reshape(KT, P, SSM_HEADS).transpose(1, 0, 2).reshape(P, -1)

    def feature_major(v):
        return v[0].T.reshape(KT, P, TOK).transpose(1, 0, 2).reshape(P, KT * TOK)

    c_f32, c_bf = constants()
    arrays = dict(xT=feature_major(a["x"]), ctxT=feature_major(a["ctx"]), params=params, heads_row=heads_row,
                  ssm_cols=ssm_cols, dskip=dskip, stream=stream, dt_w=dt_w, c_f32=c_f32, c_bf=c_bf)
    arrays = {k: np.ascontiguousarray(v) for k, v in arrays.items()}
    nc = _bacc.Bacc("TRN2", target_bir_lowering=False, num_devices=1)
    args = {k: nc.dram_tensor(k, v.shape, mybir.dt.from_np(v.dtype), kind="ExternalInput").ap()
            for k, v in arrays.items()}
    out = nc.dram_tensor("out", (P, KT * TOK), F32, kind="ExternalOutput").ap()
    build(nc, out=out, **args)
    r = _run(nc, [arrays], core_ids=[0])
    y = r.results[0]["out"].reshape(P, KT, TOK).transpose(2, 1, 0).reshape(1, TOK, D)
    return np.ascontiguousarray(y)
```
